# Optimizing a Trainium2 kernel written in Bass

```python
import jax, jax.numpy as jnp
from jax import lax
import numpy as np

D_MODEL = 2048
BATCH = 1
SEQ = 256
DEPTH = 2

HEAD_DIM = 128
BLOCK = 128
A_HEADS = D_MODEL // (2 * HEAD_DIM)
DILATED_GROUPS = ((128, 1), (512, 4), (2048, 16))
B_HEADS = D_MODEL // (2 * HEAD_DIM)
MLA_Q_LORA = 512
MLA_KV_LORA = 256
MLA_NOPE = 128
MLA_ROPE = 64
MLA_V = 128
C_HEADS = D_MODEL // HEAD_DIM
PEER_HEADS = 8
PEER_N_KEYS = 128
PEER_N_EXPERTS = PEER_N_KEYS * PEER_N_KEYS
PEER_TOPK = 16
PEER_QUERY_DIM = 256
PEER_HALF = PEER_QUERY_DIM // 2
PEER_CHUNK = 128
ROPE_THETA = 10000.0
LN_EPS = 1e-5
RMS_EPS = 1e-6
NEG_INF = -1e30
DN_ALPHA = (2 * DEPTH) ** 0.25
DN_BETA = (8 * DEPTH) ** -0.25
N_EVEN = (DEPTH + 1) // 2
N_ODD = DEPTH // 2
A_QKV = 3 * A_HEADS * HEAD_DIM
EVEN_IN = A_QKV + MLA_Q_LORA + MLA_KV_LORA + MLA_ROPE
EVEN_MIX = A_HEADS * HEAD_DIM + B_HEADS * MLA_V
ODD_IN = 3 * C_HEADS * HEAD_DIM
ODD_MIX = C_HEADS * HEAD_DIM

kernel_name = "hybrid_dilated_mla_stickbreak_peer_deepnorm"

def layer_norm(x, g, b):
    xf = x.astype(jnp.float32)
    mu = jnp.mean(xf, -1, keepdims=True)
    var = jnp.mean(jnp.square(xf - mu), -1, keepdims=True)
    y = (xf - mu) * lax.rsqrt(var + LN_EPS)
    return (y * g.astype(jnp.float32) + b.astype(jnp.float32)).astype(x.dtype)

def rms_norm(x, g):
    xf = x.astype(jnp.float32)
    y = xf * lax.rsqrt(jnp.mean(jnp.square(xf), -1, keepdims=True) + RMS_EPS)
    return (y * g.astype(jnp.float32)).astype(x.dtype)

def rope(x, pos):
    half = x.shape[-1] // 2
    inv = ROPE_THETA ** (-jnp.arange(half, dtype=jnp.float32) / half)
    ang = pos.astype(jnp.float32)[:, None] * inv[None, :]
    cos = jnp.cos(ang)[None, :, None, :]
    sin = jnp.sin(ang)[None, :, None, :]
    xf = x.astype(jnp.float32)
    x1, x2 = xf[..., :half], xf[..., half:]
    return jnp.concatenate([x1 * cos - x2 * sin, x1 * sin + x2 * cos], -1).astype(x.dtype)

def dilated_window_attention(q, k, v, dilation, steps):
    B, S, H, Dh = q.shape
    L = S // dilation
    Lp = -(-L // BLOCK) * BLOCK
    nb = Lp // BLOCK

    def to_sub(t):
        t = t.reshape(B, L, dilation, H, Dh).transpose(0, 2, 3, 1, 4)
        t = jnp.pad(t, ((0, 0), (0, 0), (0, 0), (0, Lp - L), (0, 0)))
        return t.reshape(B, dilation, H, nb, BLOCK, Dh)

    def with_prev(t):
        prev = jnp.pad(t, ((0, 0), (0, 0), (0, 0), (1, 0), (0, 0), (0, 0)))[:, :, :, :-1]
        return jnp.concatenate([prev, t], axis=4)

    qs = to_sub(q)
    kk = with_prev(to_sub(k))
    vv = with_prev(to_sub(v))
    logits = jnp.einsum('brhnqd,brhnkd->brhnqk', qs, kk).astype(jnp.float32) * (Dh ** -0.5)
    a = jnp.arange(BLOCK)[:, None]
    c = jnp.arange(2 * BLOCK)[None, :]
    rel = a + BLOCK - c
    band = (rel >= 0) & (rel <= steps)
    valid = (jnp.arange(nb)[:, None, None] > 0) | (c[None] >= BLOCK)
    mask = band[None] & valid
    logits = jnp.where(mask, logits, NEG_INF)
    m = jnp.max(logits, -1, keepdims=True)
    p = jnp.exp(logits - m)
    denom = jnp.sum(p, -1, keepdims=True)
    out = jnp.einsum('brhnqk,brhnkd->brhnqd', (p / denom).astype(v.dtype), vv)
    lse = (m + jnp.log(denom))[..., 0]
    out = out.reshape(B, dilation, H, Lp, Dh)[:, :, :, :L].transpose(0, 3, 1, 2, 4).reshape(B, S, H, Dh)
    lse = lse.reshape(B, dilation, H, Lp)[..., :L].transpose(0, 3, 1, 2).reshape(B, S, H)
    return out, lse

def causal_block_attention(q, k, v, scale):
    B, S, H, dq = q.shape
    nb = S // BLOCK
    qb = q.reshape(B, nb, BLOCK, H, dq).transpose(1, 0, 2, 3, 4)
    starts = jnp.arange(nb) * BLOCK
    kpos = jnp.arange(S)

    def one(args):
        qc, start = args
        s = jnp.einsum('bqhd,bkhd->bhqk', qc, k).astype(jnp.float32) * scale
        mask = kpos[None, :] <= (start + jnp.arange(BLOCK))[:, None]
        p = jax.nn.softmax(jnp.where(mask, s, NEG_INF), axis=-1)
        return jnp.einsum('bhqk,bkhd->bqhd', p.astype(v.dtype), v)

    out = lax.map(one, (qb, starts))
    return out.transpose(1, 0, 2, 3, 4).reshape(B, S, H, v.shape[-1])

def stick_breaking_attention(q, k, v):
    B, S, H, Dh = q.shape
    nb = S // BLOCK
    qb = q.reshape(B, nb, BLOCK, H, Dh).transpose(1, 0, 2, 3, 4)
    starts = jnp.arange(nb) * BLOCK
    kpos = jnp.arange(S)
    scale = Dh ** -0.5

    def one(args):
        qc, start = args
        z = jnp.einsum('bqhd,bkhd->bhqk', qc, k).astype(jnp.float32) * scale
        mask = kpos[None, :] < (start + jnp.arange(BLOCK))[:, None]
        log_beta = jax.nn.log_sigmoid(z)
        log_rest = jnp.where(mask, jax.nn.log_sigmoid(-z), 0.0)
        suffix = lax.cumsum(log_rest, axis=3, reverse=True) - log_rest
        att = jnp.where(mask, jnp.exp(log_beta + suffix), 0.0)
        return jnp.einsum('bhqk,bkhd->bqhd', att.astype(v.dtype), v)

    out = lax.map(one, (qb, starts))
    return out.transpose(1, 0, 2, 3, 4).reshape(B, S, H, Dh)

def even_mixer(x, w_in, q_norm, w_q_b, kv_norm, w_kv_b, w_out):
    B, S, _ = x.shape
    pos = jnp.arange(S)
    h = x @ w_in
    o1 = A_QKV
    o2 = o1 + MLA_Q_LORA
    o3 = o2 + MLA_KV_LORA
    qkv = h[..., :o1].reshape(B, S, 3, A_HEADS, HEAD_DIM)
    qa = rope(qkv[:, :, 0], pos)
    ka = rope(qkv[:, :, 1], pos)
    va = qkv[:, :, 2]
    outs, lses = [], []
    for window, dil in DILATED_GROUPS:
        o, l = dilated_window_attention(qa, ka, va, dil, window // dil)
        outs.append(o)
        lses.append(l)
    wts = jax.nn.softmax(jnp.stack(lses, 0), axis=0)
    out_a = jnp.sum(wts[..., None] * jnp.stack(outs, 0).astype(jnp.float32), 0).astype(x.dtype)
    c_q = rms_norm(h[..., o1:o2], q_norm)
    q = (c_q @ w_q_b).reshape(B, S, B_HEADS, MLA_NOPE + MLA_ROPE)
    q = jnp.concatenate([q[..., :MLA_NOPE], rope(q[..., MLA_NOPE:], pos)], -1)
    c_kv = rms_norm(h[..., o2:o3], kv_norm)
    kv = (c_kv @ w_kv_b).reshape(B, S, B_HEADS, MLA_NOPE + MLA_V)
    k_rope = rope(h[..., o3:].reshape(B, S, 1, MLA_ROPE), pos)
    k = jnp.concatenate([kv[..., :MLA_NOPE], jnp.broadcast_to(k_rope, (B, S, B_HEADS, MLA_ROPE))], -1)
    out_b = causal_block_attention(q, k, kv[..., MLA_NOPE:], (MLA_NOPE + MLA_ROPE) ** -0.5)
    cat = jnp.concatenate([out_a.reshape(B, S, -1), out_b.reshape(B, S, -1)], -1)
    return cat @ w_out

def odd_mixer(x, w_in, w_out):
    B, S, _ = x.shape
    qkv = (x @ w_in).reshape(B, S, 3, C_HEADS, HEAD_DIM)
    o = stick_breaking_attention(qkv[:, :, 0], qkv[:, :, 1], qkv[:, :, 2])
    return o.reshape(B, S, -1) @ w_out

def peer(x, w_query, sub_keys, u_table, v_table):
    B, S, D = x.shape
    xt = x.reshape(-1, PEER_CHUNK, D)

    def chunk(xc):
        T = xc.shape[0]
        q = (xc @ w_query).reshape(T, PEER_HEADS, 2, PEER_HALF)
        s1 = jnp.einsum('thk,hnk->thn', q[:, :, 0], sub_keys[:, 0]).astype(jnp.float32)
        s2 = jnp.einsum('thk,hnk->thn', q[:, :, 1], sub_keys[:, 1]).astype(jnp.float32)
        v1, i1 = lax.top_k(s1, PEER_TOPK)
        v2, i2 = lax.top_k(s2, PEER_TOPK)
        cand = (v1[..., :, None] + v2[..., None, :]).reshape(T, PEER_HEADS, PEER_TOPK * PEER_TOPK)
        cand_idx = (i1[..., :, None] * PEER_N_KEYS + i2[..., None, :]).reshape(T, PEER_HEADS, -1)
        top_s, sel = lax.top_k(cand, PEER_TOPK)
        idx = jnp.take_along_axis(cand_idx, sel, axis=-1)
        g = jax.nn.softmax(top_s, axis=-1)
        u = u_table[idx]
        act = jax.nn.gelu(jnp.einsum('thkd,td->thk', u, xc).astype(jnp.float32), approximate=False)
        vsel = v_table[idx]
        return jnp.einsum('thk,thkd->td', (g * act).astype(x.dtype), vsel)

    return lax.map(chunk, xt).reshape(B, S, D)

def setup_inputs(seed: int = 0) -> dict:
    key = jax.random.key(seed)
    ks = jax.random.split(key, 16)
    f32 = jnp.float32

    def nrm(k, shape, scale):
        return jax.random.normal(k, shape, f32) * scale

    return {
        "x": nrm(ks[0], (BATCH, SEQ, D_MODEL), 1.0),
        "a_w_in": nrm(ks[1], (N_EVEN, D_MODEL, EVEN_IN), D_MODEL ** -0.5),
        "b_q_norm": 1.0 + nrm(ks[2], (N_EVEN, MLA_Q_LORA), 0.01),
        "b_w_q_b": nrm(ks[3], (N_EVEN, MLA_Q_LORA, B_HEADS * (MLA_NOPE + MLA_ROPE)), MLA_Q_LORA ** -0.5),
        "b_kv_norm": 1.0 + nrm(ks[4], (N_EVEN, MLA_KV_LORA), 0.01),
        "b_w_kv_b": nrm(ks[5], (N_EVEN, MLA_KV_LORA, B_HEADS * (MLA_NOPE + MLA_V)), MLA_KV_LORA ** -0.5),
        "ab_w_out": nrm(ks[6], (N_EVEN, EVEN_MIX, D_MODEL), DN_BETA * EVEN_MIX ** -0.5),
        "c_w_in": nrm(ks[7], (N_ODD, D_MODEL, ODD_IN), D_MODEL ** -0.5),
        "c_w_out": nrm(ks[8], (N_ODD, ODD_MIX, D_MODEL), DN_BETA * ODD_MIX ** -0.5),
        "peer_w_query": nrm(ks[9], (DEPTH, D_MODEL, PEER_HEADS * PEER_QUERY_DIM), D_MODEL ** -0.5),
        "peer_sub_keys": nrm(ks[10], (DEPTH, PEER_HEADS, 2, PEER_N_KEYS, PEER_HALF), PEER_HALF ** -0.5),
        "peer_u": nrm(ks[11], (DEPTH, PEER_N_EXPERTS, D_MODEL), D_MODEL ** -0.5),
        "peer_v": nrm(ks[12], (DEPTH, PEER_N_EXPERTS, D_MODEL), DN_BETA),
        "ln_gain": 1.0 + nrm(ks[13], (DEPTH, 2, D_MODEL), 0.01),
        "ln_bias": nrm(ks[14], (DEPTH, 2, D_MODEL), 0.01),
    }

def reference(x, a_w_in, b_q_norm, b_w_q_b, b_kv_norm, b_w_kv_b, ab_w_out, c_w_in, c_w_out,
              peer_w_query, peer_sub_keys, peer_u, peer_v, ln_gain, ln_bias):
    for layer in range(DEPTH):
        i = layer // 2
        if layer % 2 == 0:
            mix = even_mixer(x, a_w_in[i], b_q_norm[i], b_w_q_b[i], b_kv_norm[i], b_w_kv_b[i], ab_w_out[i])
        else:
            mix = odd_mixer(x, c_w_in[i], c_w_out[i])
        x = layer_norm(DN_ALPHA * x + mix, ln_gain[layer, 0], ln_bias[layer, 0])
        ffn = peer(x, peer_w_query[layer], peer_sub_keys[layer], peer_u[layer], peer_v[layer])
        x = layer_norm(DN_ALPHA * x + ffn, ln_gain[layer, 1], ln_bias[layer, 1])
    return x


_drawn_inputs = setup_inputs


def setup_inputs(seed=0):
    import zlib

    import numpy as np

    out = dict(_drawn_inputs(seed))
    spreads = {}
    factors = {'b_q_norm': 5.438, 'b_kv_norm': 4.971}
    for name, (base, spread) in spreads.items():
        noise = np.random.default_rng([zlib.crc32(name.encode()), seed]).standard_normal(out[name].shape)
        drawn = base * np.exp(spread * noise) if base else spread * noise
        out[name] = __import__('jax').numpy.asarray(drawn.astype(out[name].dtype))
    for name, factor in factors.items():
        out[name] = (out[name] * factor).astype(out[name].dtype)
    return out
```

```python
from contextlib import ExitStack

import concourse.bass as bass
import concourse.mybir as mybir
import numpy as np
from concourse.alu_op_type import AluOpType as ALU

ACT = mybir.ActivationFunctionType
AX = mybir.AxisListType
F32 = mybir.dt.float32
F32R = mybir.dt.float32r
U32 = mybir.dt.uint32

P = 128
D = 2048
T = 256
TILES = T // P
KC = D // P
UNIT = 1024
STAGES = 4
SPLITS = 2
HEADS = 8
C_HEADS = 16
TOPK = 16
N_KEYS = 128
Q_LORA = 512
KV_LORA = 256
ROPE = 64
ALPHA = float(4 ** 0.25)
LN_EPS = 1e-5
RMS_EPS = 1e-6
NEG = -1e30
REPLACED = -3.0e38
A_SCALE = float(128 ** -0.5)
B_SCALE = float((128 + 64) ** -0.5)
QUARTER = KC // 4


class At:

    def __init__(self, c, i=None, step=0):
        self.c, self.i, self.step = c, i, step

    def plus(self, n):
        return At(self.c + n, self.i, self.step)

    def times(self, n):
        return At(self.c * n, self.i, self.step * n)

    def index(self):
        return self.c if self.i is None else self.i * self.step + self.c

    def slot(self, ring):
        return self.c % ring

    def turn(self, ring, more=0, each=1):
        c = (self.c // ring + more) * each
        return c if self.i is None else self.i * (self.step // ring * each) + c


def repeat(eng, first, last, step, body, peel=0):
    for c in range(first, first + peel):
        body(At(c))
    first += peel
    n = (last - first) // step
    if n >= 2:
        with eng.Fori(0, n) as i:
            for r in range(step):
                body(At(first + r, i, step))
        first += n * step
    for c in range(first, last):
        body(At(c))


def wait_round(eng, s, turns):
    if not isinstance(turns, int) or turns > 0:
        eng.wait_ge(s, turns)


def decoder(nc, t):
    with ExitStack() as ctx:
        def sb(name, shape, dt=F32):
            return ctx.enter_context(nc.sbuf_tensor(name, shape, dt))

        sems = {}

        def sem(name):
            if name not in sems:
                sems[name] = ctx.enter_context(nc.semaphore(name))
            return sems[name]

        arena = sb("arena", [P, P, T])
        xT = sb("xT", [P, KC, 2, T], F32R)
        stage = sb("stage", [P, STAGES, UNIT])
        w_hi = sb("w_hi", [P, SPLITS, UNIT], F32R)
        w_lo = sb("w_lo", [P, SPLITS, UNIT], F32R)
        half_sum = sb("half_sum", [P, 2, T])
        const = sb("const", [P, 5, P])
        picks = sb("picks", [P, 3, T])
        onehot = sb("onehot", [P, 2, 2, 2, P])
        small = sb("small", [P, 224])
        ps = ctx.enter_context(nc.psum_tensor("ps", [P, 8, 512], F32))

        ident, ones, iota, rot_a, rot_b = (const[:, k, :] for k in range(5))
        q_gain, kv_gain = small[:, 0:4], small[:, 4:6]
        mean_var = small[:, 8:12].rearrange("p (m k) -> p m k", m=2)
        rstd = small[:, 12:14]
        bn = small[:, 16:64].rearrange("p (m c k) -> p m c k", m=2, c=4)
        neg_max = small[:, 64:96].rearrange("p (h m) -> p h m", m=2)
        row_sum = small[:, 96:128].rearrange("p (h m) -> p h m", m=2)
        inv_sum = small[:, 128:160].rearrange("p (h m) -> p h m", m=2)
        neg_top = small[:, 160:168]
        gate_sum = small[:, 168:176]
        gate_inv = small[:, 176:184]
        ln_eps, rms_eps = small[:, 184:185], small[:, 185:186]

        def blocks(first, count):
            return arena[:, first:first + count, :].rearrange("p b t -> p (b t)")

        residual = blocks(0, 16).rearrange("p (m d) -> p m d", m=2)
        gain, bias = blocks(16, 8), blocks(24, 8)
        RAW, Q_AT, K_AT, CQ_AT, CKV_AT, KR_AT = 0, 0, 8, 16, 20, 22
        val_a = blocks(23, 8).rearrange("p (m d) -> p m d", m=2)
        x_first = blocks(31, 16).rearrange("p (m d) -> p m d", m=2)
        CQN, CKVN, QB, KN = 31, 35, 37, 49
        val_b = blocks(57, 8).rearrange("p (m d) -> p m d", m=2)
        w_qb = blocks(65, 24).rearrange("p (k n) -> p k n", k=4)
        w_kvb = blocks(89, 16).rearrange("p (k n) -> p k n", k=2)
        even_masks = blocks(105, 5)[:, 0:1152].rearrange("p (k n) -> p k n", k=3)
        trig = arena[:, 110:114, :]
        probs = blocks(114, 3).rearrange("p (r n) -> p r n", r=2)
        probs_t = blocks(117, 3).rearrange("p (r n) -> p r n", r=2)
        squares = blocks(120, 6)
        rms = arena[:, 126:128, :]
        rotated = blocks(120, 4).rearrange("p (r n) -> p r n", r=2)
        OQ_AT, OK_AT = 0, 16
        val_c = blocks(32, 16).rearrange("p (m d) -> p m d", m=2)
        odd_consts = blocks(48, 3)
        tri, diag_mask, neg_mask = odd_consts[:, 0:128], odd_consts[:, 128:256], odd_consts[:, 256:640]

        def ring2(first):
            return blocks(first, 3).rearrange("p (r n) -> p r n", r=2)

        z_abs, z_exp, z_log, z_max, log_rest, att = (ring2(51 + 3 * k) for k in range(6))
        QT_AT = 32
        keys_t = blocks(48, 8).rearrange("p (s n) -> p s n", s=16)
        scores = blocks(56, 8).rearrange("p (s n) -> p s n", s=16)
        scores_cut = blocks(64, 8).rearrange("p (s n) -> p s n", s=16)
        top_v = arena[:, 72, :].rearrange("p (s k) -> p s k", s=16)
        top_i = arena[:, 73, :].bitcast(U32).rearrange("p (s k) -> p s k", s=16)
        top_f = arena[:, 74, :].rearrange("p (s k) -> p s k", s=16)
        cand = blocks(75, 8).rearrange("p (h n) -> p h n", h=HEADS)
        cand_cut = blocks(83, 8).rearrange("p (h n) -> p h n", h=HEADS)
        best_v = arena[:, 91, 0:128].rearrange("p (h k) -> p h k", h=HEADS)
        best_i = arena[:, 91, 128:256].bitcast(U32).rearrange("p (h k) -> p h k", h=HEADS)
        rank_i = arena[:, 92, :].bitcast(U32).rearrange("p (s n) -> p s n", s=2)
        rank_f = arena[:, 93, :].rearrange("p (s n) -> p s n", s=2)
        match = blocks(94, 8)
        picked = blocks(102, 2)[:, 0:384].rearrange("p (w n) -> p w n", w=3)
        best_sh = arena[:, 104, 0:128].rearrange("p (h k) -> p h k", h=HEADS)
        gates_by_group = arena[:, :, :].rearrange("p i (g t) -> p i g t", t=4)

        order = [("even_in", "even_in"), ("even_v", "even_v"), ("even_out", "even_out"),
                 ("query0", "query0"), ("u0", "u0"), ("v0", "v0"),
                 ("odd_in", "odd_in"), ("odd_v", "odd_v"), ("odd_out", "odd_out"),
                 ("query1", "query1"), ("u1", "u1"), ("v1", "v1")]
        base, at = {}, 0
        for name, _ in order:
            base[name] = at
            at += t[name].shape[0]
        FEATURE = ["even_in", "query0", "u0", "odd_in", "query1", "u1"]
        first_block, at = {}, 0
        for name in FEATURE:
            first_block[name] = at
            at += t[name].shape[0] // 2

        def n_blocks(name):
            return t[name].shape[0] // 2

        staged = [sem(f"staged{s}") for s in range(STAGES)]
        hi_ready = [sem(f"hi_ready{s}") for s in range(STAGES)]
        lo_ready = [sem(f"lo_ready{s}") for s in range(STAGES)]
        used = [sem(f"used{s}") for s in range(SPLITS)]
        half_ready = [sem(f"half_ready{s}") for s in range(2)]
        bank_free = [sem(f"bank_free{s}") for s in range(2)]

        block = ctx.enter_context(nc.Block())

        @block.sync
        def _(sp):
            for name, _ in order:
                units = t[name]

                def load(a, units=units, name=name):
                    g = a.plus(base[name])
                    wait_round(sp, lo_ready[g.slot(STAGES)], g.turn(STAGES))
                    sp.dma_start(stage[:, g.slot(STAGES), :], units[a.index()]).then_inc(
                        staged[g.slot(STAGES)], 16)

                repeat(sp, 0, units.shape[0], STAGES, load, peel=0 if base[name] else STAGES)

        @block.gpsimd
        def _(pool):
            def get(dst, src, s):
                pool.dma_start(dst, src).then_inc(sem(s), 16)

            get(x_first, t["x"].rearrange("(m p) d -> p m d", p=P), "x_in")
            get(const[:, :, :], t["const"], "const_in")
            get(q_gain, t["q_gain"], "mla_in")
            get(kv_gain, t["kv_gain"], "mla_in")
            get(w_qb, t["w_qb"], "mla_in")
            get(w_kvb, t["w_kvb"], "mla_in")
            get(even_masks, t["even_masks"], "mla_in")
            get(trig, t["trig"], "mla_in")

            def norm_in(k, source):
                get(residual, source, f"ln_in{k}")
                get(gain, t["ln_gain"][k].partition_broadcast(P), f"ln_in{k}")
                get(bias, t["ln_bias"][k].partition_broadcast(P), f"ln_in{k}")

            def keep(k):
                pool.wait_ge(sem(f"ln_done{k}"), 1)
                get(t["kept"][k].rearrange("(m p) d -> p m d", p=P), residual, f"kept{k}")
                pool.wait_ge(sem(f"kept{k}"), 16)

            pool.wait_ge(sem("heads_lo0"), 16)
            norm_in(0, t["x"].rearrange("(m p) d -> p m d", p=P))
            for layer in range(2):
                keep(2 * layer)
                pool.wait_ge(sem(f"qT_ready{layer}"), 1)
                get(keys_t, t["keys_t"][layer], f"keys_in{layer}")
                pool.wait_ge(sem(f"h_lo{layer}"), 33)
                norm_in(2 * layer + 1, t["kept"][2 * layer].rearrange("(m p) d -> p m d", p=P))
                if layer == 0:
                    keep(1)
                    pool.wait_ge(sem("pe_v_done0"), 1)
                    get(odd_consts[:, 0:640], t["odd_consts"], "odd_in")
                    pool.wait_ge(sem("heads_lo1"), 16)
                    norm_in(2, t["kept"][1].rearrange("(m p) d -> p m d", p=P))
            pool.wait_ge(sem("ln_done3"), 1)
            get(t["out"].rearrange("(m p) d -> p m d", p=P), residual, "out_done")
            pool.wait_ge(sem("out_done"), 16)

        @block.scalar
        def _(act):
            def split_hi(g):
                act.wait_ge(staged[g.slot(STAGES)], g.turn(STAGES, 1, 16))
                wait_round(act, used[g.slot(SPLITS)], g.turn(SPLITS))
                nc.scalar.activation(w_hi[:, g.slot(SPLITS), :], stage[:, g.slot(STAGES), :],
                                     ACT.Copy).then_inc(hi_ready[g.slot(STAGES)], 1)

            def token_splits(name):
                repeat(act, base[name], base[name] + t[name].shape[0], STAGES, split_hi)

            def copy_half(name, b):
                last = b.times(2).plus(base[name] + 1)
                act.wait_ge(used[last.slot(SPLITS)], last.turn(SPLITS, 1))
                k = b.plus(first_block[name])
                nc.scalar.activation(half_sum[:, k.slot(2), :], ps[:, k.slot(2), T:2 * T],
                                     ACT.Copy).then_inc(half_ready[k.slot(2)], 1)

            def gelu(layer, b):
                nc.scalar.activation(arena[:, b.index(), :], arena[:, b.index(), :],
                                     ACT.Gelu).then_inc(sem(f"gelu{layer}"), 1)

            def feature(name, layer=None):
                n = n_blocks(name)

                def splits(b):
                    split_hi(b.times(2).plus(base[name]))
                    split_hi(b.times(2).plus(base[name] + 1))

                def with_copy(b):
                    splits(b)
                    copy_half(name, b.plus(-1))

                def with_gelu(b):
                    splits(b)
                    before = b.plus(first_block[name] - 2)
                    act.wait_ge(bank_free[before.slot(2)], before.turn(2, 1))
                    copy_half(name, b.plus(-1))
                    gelu(layer, b.plus(-2))

                splits(At(0))
                if layer is None:
                    repeat(act, 1, n, 2, with_copy)
                    copy_half(name, At(n - 1))
                else:
                    with_copy(At(1))
                    repeat(act, 2, n, 2, with_gelu)
                    copy_half(name, At(n - 1))
                    for b in (n - 2, n - 1):
                        k = At(b + first_block[name])
                        act.wait_ge(bank_free[k.slot(2)], k.turn(2, 1))
                        gelu(layer, At(b))

            def x_hi(k):
                for g in range(8):
                    m, q = divmod(g, 4)
                    act.wait_ge(sem(f"xt_ps{k}"), g + 1)
                    nc.scalar.activation(
                        xT[:, 4 * q:4 * q + 4, 0, m * P:(m + 1) * P],
                        ps[:, 2 + g % 2, :].rearrange("p (c t) -> p c t", c=4),
                        ACT.Copy).then_inc(sem(f"xt_hi{k}"), 1)

            def ln_std(k):
                act.wait_ge(sem(f"ln_stats{k}"), 1)
                nc.scalar.activation(rstd, mean_var[:, :, 1], ACT.Sqrt, bias=ln_eps).then_inc(
                    sem(f"ln_std{k}"), 1)

            def latent():
                b22 = first_block["even_in"] + n_blocks("even_in") - 1
                act.wait_ge(bank_free[b22 % 2], b22 // 2 + 1)
                act.wait_ge(bank_free[(b22 - 1) % 2], (b22 - 1) // 2 + 1)
                nc.scalar.activation(squares, blocks(CQ_AT, 6), ACT.Square).then_inc(sem("sq"), 1)
                act.wait_ge(sem("sq_ps"), 1)
                act.wait_ge(sem("eps_set"), 1)
                nc.scalar.activation(rms[:, 0, :], ps[:, 2, 0:T], ACT.Sqrt, bias=rms_eps,
                                     scale=1.0 / Q_LORA)
                nc.scalar.activation(rms[:, 1, :], ps[:, 2, T:2 * T], ACT.Sqrt, bias=rms_eps,
                                     scale=1.0 / KV_LORA).then_inc(sem("rms_std"), 1)
                for n in range(14):
                    act.wait_ge(sem("mla_ps"), n + 1)
                    if n < 10:
                        dst = blocks((QB if n < 6 else KN - 12) + 2 * n, 2)
                    else:
                        m, c = divmod(n - 10, 2)
                        dst = val_b[:, m, 512 * c:512 * c + 512]
                    nc.scalar.activation(dst, ps[:, 2 + n % 2, :], ACT.Copy).then_inc(sem("mla_out"), 1)

            def soft_exp(h):
                act.wait_ge(sem("max_ready"), h + 1)
                for m in range(2):
                    e = probs[:, h % 2, 128 * m:128 + 256 * m]
                    kw = {"accum_out": row_sum[:, h, m:m + 1]} if h >= HEADS else {}
                    last = nc.scalar.activation(e, e, ACT.Exp, bias=neg_max[:, h, m:m + 1], **kw)
                last.then_inc(sem("exp_ready"), 1)

            def probs_out(h):
                act.wait_ge(sem("turned_ps"), h + 1)
                if h >= 2:
                    act.wait_ge(sem("head_ps0"), h - 1)
                nc.scalar.activation(probs_t[:, h % 2, :], ps[:, 4 + h % 2, 0:384],
                                     ACT.Copy).then_inc(sem("turned"), 1)

            def head_hi(layer, h):
                act.wait_ge(sem(f"head_ps{layer}"), h + 1)
                nc.scalar.activation(xT[:, h, 0, :], ps[:, 6 + h % 2, 0:T], ACT.Copy).then_inc(
                    sem(f"heads_hi{layer}"), 1)

            def stick_logs(h):
                r = h % 2
                act.wait_ge(sem("z_ps"), h + 1)
                nc.scalar.activation(z_abs[:, r, :], ps[:, 2 + r, 0:384], ACT.Abs).then_inc(
                    sem("abs_ready"), 1)
                act.wait_ge(sem("abs_ready"), h + 1)
                nc.scalar.activation(z_exp[:, r, :], z_abs[:, r, :], ACT.Exp, scale=-1.0).then_inc(
                    sem("zexp_ready"), 1)
                act.wait_ge(sem("zexp_ready"), h + 1)
                if h >= 2:
                    act.wait_ge(sem("rest_ready"), h - 1)
                nc.scalar.activation(z_log[:, r, :], z_exp[:, r, :], ACT.Ln, bias=1.0).then_inc(
                    sem("log_ready"), 1)

            def stick_att(h):
                act.wait_ge(sem("suffix_ps"), h + 1)
                if h >= 2:
                    act.wait_ge(sem("head_ps1"), h - 1)
                nc.scalar.activation(att[:, h % 2, :], ps[:, 4 + h % 2, 0:384], ACT.Exp).then_inc(
                    sem("att_ready"), 1)

            def retrieve(layer):
                for m in range(2):
                    for g in range(4):
                        n = 4 * m + g
                        act.wait_ge(sem(f"score_ps{layer}"), n + 1)
                        if m:
                            act.wait_ge(sem(f"picks_done{layer}"), 1)
                        nc.scalar.activation(
                            scores[:, 4 * g:4 * g + 4, :].rearrange("p s n -> p (s n)"),
                            ps[:, 2 + n % 2, :], ACT.Copy).then_inc(sem(f"scores{layer}"), 1)
                    act.wait_ge(sem(f"shifted{layer}"), m + 1)
                    for h in range(HEADS):
                        last = nc.scalar.activation(picked[:, 2, TOPK * h:TOPK * h + TOPK],
                                                    best_sh[:, h, :], ACT.Exp,
                                                    accum_out=gate_sum[:, h:h + 1])
                    last.then_inc(sem(f"gate_exp{layer}"), 1)
                    act.wait_ge(sem(f"picks_ps{layer}"), m + 1)
                    nc.scalar.activation(picks[:, :, m * P:(m + 1) * P],
                                         ps[:, 4, 0:384].rearrange("p (w t) -> p w t", w=3),
                                         ACT.Copy).then_inc(sem(f"picks_T{layer}"), 1)

            def values(layer):
                name = f"v{layer}"

                def row(b):
                    split_hi(b.times(2).plus(base[name]))
                    nc.scalar.activation(xT[:, b.slot(2), 0, :], arena[:, b.index(), :],
                                         ACT.Copy).then_inc(sem(f"h_hi{layer}"), 1)
                    split_hi(b.times(2).plus(base[name] + 1))

                act.wait_ge(sem(f"gated{layer}"), 1)
                repeat(act, 0, P, 2, row)

            x_hi(0)
            feature("even_in")
            token_splits("even_v")
            for n in range(4):
                act.wait_ge(sem("va_ps"), 1)
                m, c = divmod(n, 2)
                last = nc.scalar.activation(val_a[:, m, 512 * c:512 * c + 512], ps[:, 4 + n, :],
                                            ACT.Copy)
            last.then_inc(sem("va_out"), 1)
            latent()
            soft_exp(0)
            for h in range(2 * HEADS):
                if h + 1 < 2 * HEADS:
                    soft_exp(h + 1)
                probs_out(h)
                if h:
                    head_hi(0, h - 1)
            head_hi(0, 2 * HEADS - 1)
            token_splits("even_out")
            ln_std(0)
            x_hi(1)
            for layer in range(2):
                feature(f"query{layer}")
                retrieve(layer)
                feature(f"u{layer}", layer)
                values(layer)
                ln_std(2 * layer + 1)
                if layer == 0:
                    x_hi(2)
                    feature("odd_in")
                    token_splits("odd_v")
                    for n in range(8):
                        act.wait_ge(sem("vc_ps"), 1)
                        m, c = divmod(n, 4)
                        last = nc.scalar.activation(val_c[:, m, 512 * c:512 * c + 512],
                                                    ps[:, n, :], ACT.Copy)
                    last.then_inc(sem("vc_out"), 1)
                    stick_logs(0)
                    for h in range(C_HEADS):
                        if h + 1 < C_HEADS:
                            stick_logs(h + 1)
                        stick_att(h)
                        if h:
                            head_hi(1, h - 1)
                    head_hi(1, C_HEADS - 1)
                    token_splits("odd_out")
                    ln_std(2)
                    x_hi(3)

        @block.vector
        def _(dve):
            count = [0]

            def settle(ins):
                count[0] += 1
                ins.then_inc(sem("dve_steps"), 1)
                dve.wait_ge(sem("dve_steps"), count[0])

            def split_lo(g):
                dve.wait_ge(hi_ready[g.slot(STAGES)], g.turn(STAGES, 1))
                nc.vector.tensor_tensor(w_lo[:, g.slot(SPLITS), :], stage[:, g.slot(STAGES), :],
                                        w_hi[:, g.slot(SPLITS), :].bitcast(F32),
                                        ALU.subtract).then_inc(lo_ready[g.slot(STAGES)], 1)

            def token_splits(name):
                repeat(dve, base[name], base[name] + t[name].shape[0], STAGES, split_lo)

            def add_up(name, b, dest):
                k = b.plus(first_block[name])
                dve.wait_ge(half_ready[k.slot(2)], k.turn(2, 1))
                nc.vector.tensor_tensor(arena[:, b.plus(dest).index(), :], ps[:, k.slot(2), 0:T],
                                        half_sum[:, k.slot(2), :], ALU.add).then_inc(
                                            bank_free[k.slot(2)], 1)

            def feature(name, dest):
                n = n_blocks(name)

                def splits(b):
                    split_lo(b.times(2).plus(base[name]))
                    split_lo(b.times(2).plus(base[name] + 1))

                def step(b):
                    splits(b)
                    add_up(name, b.plus(-1), dest)

                splits(At(0))
                repeat(dve, 1, n, 2, step)
                add_up(name, At(n - 1), dest)

            def all_added(name):
                for b in (n_blocks(name) - 2, n_blocks(name) - 1):
                    k = At(b + first_block[name])
                    dve.wait_ge(bank_free[k.slot(2)], k.turn(2, 1))

            def x_lo(k):
                for g in range(8):
                    m, q = divmod(g, 4)
                    dve.wait_ge(sem(f"xt_hi{k}"), g + 1)
                    nc.vector.tensor_tensor(
                        xT[:, 4 * q:4 * q + 4, 1, m * P:(m + 1) * P],
                        ps[:, 2 + g % 2, :].rearrange("p (c t) -> p c t", c=4),
                        xT[:, 4 * q:4 * q + 4, 0, m * P:(m + 1) * P].bitcast(F32),
                        ALU.subtract).then_inc(sem(f"xt_lo{k}"), 1)

            def layer_norm(k):
                dve.wait_ge(sem(f"ln_in{k}"), 48)
                dve.wait_ge(sem(f"y_ps{k}"), 8)
                for m in range(2):
                    for c in range(4):
                        part = residual[:, m, 512 * c:512 * c + 512]
                        last = nc.vector.scalar_tensor_tensor(
                            out=part, in0=part, scalar=ALPHA, in1=ps[:, 4 * m + c, :],
                            op0=ALU.mult, op1=ALU.add)
                settle(last)
                for m in range(2):
                    for c in range(4):
                        last = nc.vector.bn_stats(bn[:, m, c, :],
                                                  residual[:, m, 512 * c:512 * c + 512])
                settle(last)
                for m in range(2):
                    last = nc.vector.bn_aggr(mean_var[:, m, :],
                                             bn[:, m, :, :].rearrange("p c k -> p (c k)"))
                last.then_inc(sem(f"ln_stats{k}"), 1)
                dve.wait_ge(sem(f"ln_std{k}"), 1)
                settle(nc.vector.reciprocal(rstd, rstd))
                for m in range(2):
                    last = nc.vector.tensor_scalar(residual[:, m, :], residual[:, m, :],
                                                   mean_var[:, m, 0:1], rstd[:, m:m + 1],
                                                   ALU.subtract, ALU.mult)
                settle(last)
                for m in range(2):
                    last = nc.vector.tensor_tensor(residual[:, m, :], residual[:, m, :], gain,
                                                   ALU.mult)
                settle(last)
                for m in range(2):
                    last = nc.vector.tensor_tensor(residual[:, m, :], residual[:, m, :], bias,
                                                   ALU.add)
                last.then_inc(sem(f"ln_done{k}"), 1)

            def latent():
                dve.wait_ge(sem("mla_in"), 16 * 6)
                dve.wait_ge(sem("rms_std"), 1)
                settle(nc.vector.reciprocal(rms, rms))
                for j in range(4):
                    nc.vector.scalar_tensor_tensor(
                        out=arena[:, CQN + j, :], in0=arena[:, CQ_AT + j, :],
                        scalar=q_gain[:, j:j + 1], in1=rms[:, 0, :], op0=ALU.mult, op1=ALU.mult)
                for j in range(2):
                    last = nc.vector.scalar_tensor_tensor(
                        out=arena[:, CKVN + j, :], in0=arena[:, CKV_AT + j, :],
                        scalar=kv_gain[:, j:j + 1], in1=rms[:, 1, :], op0=ALU.mult, op1=ALU.mult)
                last.then_inc(sem("latents"), 1)

            def rotate(n, at, count, which):
                x = arena[:, at:at + count, :]
                cos, sin = (trig[:, 2 * which + k, :].unsqueeze(1).to_broadcast([P, count, T])
                            for k in range(2))
                y = rotated[:, n % 2, 0:count * T].rearrange("p (b t) -> p b t", b=count)
                dve.wait_ge(sem("rot_ps"), n + 1)
                nc.vector.tensor_tensor(
                    y, ps[:, 4 + n % 2, 0:count * T].rearrange("p (b t) -> p b t", b=count), sin,
                    ALU.mult)
                settle(nc.vector.tensor_tensor(x, x, cos, ALU.mult))
                nc.vector.tensor_tensor(x, x, y, ALU.add).then_inc(sem("roped"), 1)

            def soft_max(h):
                dve.wait_ge(sem("logit_ps"), h + 1)
                if h >= 2:
                    dve.wait_ge(sem("turned_ps"), h - 1)
                mask = even_masks[:, 1 if h < HEADS else 2, :]
                settle(nc.vector.scalar_tensor_tensor(
                    out=probs[:, h % 2, :], in0=ps[:, 2 + h % 2, 0:384],
                    scalar=A_SCALE if h < HEADS else B_SCALE, in1=mask, op0=ALU.mult, op1=ALU.add))
                for m in range(2):
                    last = nc.vector.tensor_reduce(neg_max[:, h, m:m + 1],
                                                   probs[:, h % 2, 128 * m:128 + 256 * m],
                                                   AX.X, ALU.max, negate=True)
                last.then_inc(sem("max_ready"), 1)

            def soft_norm(h):
                dve.wait_ge(sem("exp_ready"), h + 1)
                tiles = [probs[:, h % 2, 128 * m:128 + 256 * m] for m in range(2)]
                if h < HEADS:
                    for m in range(2):
                        last = nc.vector.tensor_tensor_reduce(
                            out=tiles[m], in0=tiles[m],
                            in1=even_masks[:, 0, 128 * m:128 + 256 * m], scale=1.0, scalar=0.0,
                            op0=ALU.mult, op1=ALU.add, accum_out=row_sum[:, h, m:m + 1])
                    settle(last)
                settle(nc.vector.reciprocal(inv_sum[:, h, :], row_sum[:, h, :]))
                for m in range(2):
                    last = nc.vector.tensor_scalar(tiles[m], tiles[m], inv_sum[:, h, m:m + 1], None,
                                                   ALU.mult)
                last.then_inc(sem("probs_ready"), 1)

            def head_lo(layer, h):
                dve.wait_ge(sem(f"heads_hi{layer}"), h + 1)
                nc.vector.tensor_tensor(xT[:, h, 1, :], ps[:, 6 + h % 2, 0:T],
                                        xT[:, h, 0, :].bitcast(F32), ALU.subtract).then_inc(
                                            sem(f"heads_lo{layer}"), 1)

            def stick_rest(h):
                r = h % 2
                dve.wait_ge(sem("abs_ready"), h + 1)
                nc.vector.tensor_scalar(z_max[:, r, :], ps[:, 2 + r, 0:384], 0.0, None,
                                        ALU.max).then_inc(sem("zmax_ready"), 1)
                dve.wait_ge(sem("log_ready"), h + 1)
                dve.wait_ge(sem("zmax_ready"), h + 1)
                settle(nc.vector.tensor_tensor(z_max[:, r, :], z_max[:, r, :], z_log[:, r, :],
                                               ALU.add))
                if h >= 2:
                    dve.wait_ge(sem("suffix_ps"), h - 1)
                nc.vector.tensor_tensor(log_rest[:, r, :], z_max[:, r, :], neg_mask,
                                        ALU.mult).then_inc(sem("rest_ready"), 1)

            def top16(values, cut, v, i, n):
                for s in range(n):
                    last = nc.vector.max(v[:, s, 0:8], values[:, s, :])
                settle(last)
                for s in range(n):
                    nc.vector.max_index(i[:, s, 0:8], v[:, s, 0:8], values[:, s, :])
                    last = nc.vector.match_replace(cut[:, s, :], v[:, s, 0:8], values[:, s, :],
                                                   REPLACED)
                settle(last)
                for s in range(n):
                    last = nc.vector.max(v[:, s, 8:16], cut[:, s, :])
                settle(last)
                for s in range(n):
                    last = nc.vector.max_index(i[:, s, 8:16], v[:, s, 8:16], cut[:, s, :])
                settle(last)

            def retrieve(layer):
                all_added(f"query{layer}")
                for m in range(2):
                    dve.wait_ge(sem(f"scores{layer}"), 4 * (m + 1))
                    if m:
                        dve.wait_ge(sem(f"picks_ps{layer}"), 1)
                    top16(scores, scores_cut, top_v, top_i, 16)
                    nc.vector.tensor_copy(top_f, top_i)
                    pairs = top_v.rearrange("p (h two) k -> p h two k", two=2)
                    settle(nc.vector.tensor_tensor(
                        cand.rearrange("p h (a b) -> p h a b", a=TOPK),
                        pairs[:, :, 0, :].unsqueeze(3).to_broadcast([P, HEADS, TOPK, TOPK]),
                        pairs[:, :, 1, :].unsqueeze(2).to_broadcast([P, HEADS, TOPK, TOPK]),
                        ALU.add))
                    top16(cand, cand_cut, best_v, best_i, HEADS)
                    nc.vector.tensor_tensor(best_sh, best_v,
                                            best_v[:, :, 0:1].to_broadcast([P, HEADS, TOPK]),
                                            ALU.subtract).then_inc(sem(f"shifted{layer}"), 1)
                    flat = best_i.rearrange("p h k -> p (h k)")
                    nc.vector.tensor_scalar(rank_i[:, 0, :], flat, 4, None, ALU.logical_shift_right)
                    settle(nc.vector.tensor_scalar(rank_i[:, 1, :], flat, 15, None, ALU.bitwise_and))
                    settle(nc.vector.tensor_copy(rank_f, rank_i))
                    keys = top_f.rearrange("p (h two) k -> p h two k", two=2)
                    for side in range(2):
                        eq = match.rearrange("p (n a) -> p n a", a=TOPK)
                        settle(nc.vector.tensor_tensor(
                            eq, iota[:, 0:TOPK].unsqueeze(1).to_broadcast([P, P, TOPK]),
                            rank_f[:, side, :].unsqueeze(2).to_broadcast([P, P, TOPK]),
                            ALU.is_equal))
                        by_head = match.rearrange("p (h k a) -> p h k a", h=HEADS, k=TOPK)
                        settle(nc.vector.tensor_tensor(
                            by_head, by_head,
                            keys[:, :, side, :].unsqueeze(2).to_broadcast([P, HEADS, TOPK, TOPK]),
                            ALU.mult))
                        settle(nc.vector.tensor_reduce(picked[:, side, :], eq, AX.X, ALU.add))
                    dve.wait_ge(sem(f"gate_exp{layer}"), m + 1)
                    settle(nc.vector.reciprocal(gate_inv, gate_sum))
                    g = picked[:, 2, :].rearrange("p (h k) -> p h k", h=HEADS)
                    nc.vector.tensor_tensor(g, g, gate_inv.unsqueeze(2).to_broadcast(
                        [P, HEADS, TOPK]), ALU.mult).then_inc(sem(f"picks_done{layer}"), 1)

            def gate(layer):
                def hots(pair):
                    wait_round(dve, sem(f"pair_ps{layer}_{pair.slot(2)}"), pair.turn(2))
                    for j in range(2):
                        tok = pair.times(2).plus(j).index()
                        nc.vector.tensor_scalar(
                            onehot[:, pair.slot(2), j, 0, :], iota, picks[:, 0, bass.ds(tok, 1)],
                            picks[:, 2, bass.ds(tok, 1)], ALU.is_equal, ALU.mult)
                        last = nc.vector.tensor_scalar(
                            onehot[:, pair.slot(2), j, 1, :], iota, picks[:, 1, bass.ds(tok, 1)],
                            None, ALU.is_equal)
                    last.then_inc(sem(f"hots{layer}_{pair.slot(2)}"), 1)

                def multiply(g):
                    dve.wait_ge(sem(f"pair_ps{layer}_1"), g.turn(1, 1))
                    h = gates_by_group[:, :, g.index(), :]
                    c = ps[:, 2 + g.slot(2), :].rearrange("p (t i) -> p i t", t=4)
                    nc.vector.tensor_tensor(h, c, h, ALU.mult).then_inc(
                        sem(f"group{layer}_{g.slot(2)}"), 1)

                def step(g):
                    hots(g.times(2))
                    hots(g.times(2).plus(1))
                    multiply(g.plus(-1))

                dve.wait_ge(sem(f"gelu{layer}"), P)
                hots(At(0))
                hots(At(1))
                repeat(dve, 1, T // 4, 2, step)
                multiply(At(T // 4 - 1))
                for s in range(2):
                    dve.wait_ge(sem(f"group{layer}_{s}"), T // 8)
                nc.vector.memset(small[:, 200:201], 0.0).then_inc(sem(f"gated{layer}"), 1)

            def values(layer):
                name = f"v{layer}"

                def row(b):
                    split_lo(b.times(2).plus(base[name]))
                    dve.wait_ge(sem(f"h_hi{layer}"), b.turn(1, 1))
                    nc.vector.tensor_tensor(xT[:, b.slot(2), 1, :], arena[:, b.index(), :],
                                            xT[:, b.slot(2), 0, :].bitcast(F32),
                                            ALU.subtract).then_inc(sem(f"h_lo{layer}"), 1)
                    split_lo(b.times(2).plus(base[name] + 1))

                repeat(dve, 0, P, 2, row)

            nc.vector.memset(ln_eps, LN_EPS)
            nc.vector.memset(rms_eps, RMS_EPS).then_inc(sem("eps_set"), 1)
            x_lo(0)
            feature("even_in", RAW)
            token_splits("even_v")
            latent()
            all_added("even_in")
            for n in range(8):
                rotate(n, Q_AT + 2 * n, 2, 0)
            rotate(8, KR_AT, 1, 1)
            for n in range(2):
                rotate(9 + n, QB + 8 + 2 * n, 2, 1)
            soft_max(0)
            for h in range(2 * HEADS):
                if h + 1 < 2 * HEADS:
                    soft_max(h + 1)
                soft_norm(h)
                if h:
                    head_lo(0, h - 1)
            head_lo(0, 2 * HEADS - 1)
            token_splits("even_out")
            layer_norm(0)
            x_lo(1)
            for layer in range(2):
                feature(f"query{layer}", QT_AT)
                retrieve(layer)
                dve.wait_ge(sem(f"kept{2 * layer}"), 16)
                dve.wait_ge(sem(f"picks_T{layer}"), 2)
                feature(f"u{layer}", 0)
                gate(layer)
                values(layer)
                layer_norm(2 * layer + 1)
                if layer == 0:
                    x_lo(2)
                    dve.wait_ge(sem("kept1"), 16)
                    feature("odd_in", OQ_AT)
                    all_added("odd_in")
                    q = blocks(OQ_AT, 16)
                    nc.vector.tensor_scalar(q, q, A_SCALE, None, ALU.mult).then_inc(
                        sem("q_scaled"), 1)
                    token_splits("odd_v")
                    dve.wait_ge(sem("odd_in"), 16)
                    for h in range(C_HEADS):
                        stick_rest(h)
                        if h:
                            head_lo(1, h - 1)
                    head_lo(1, C_HEADS - 1)
                    token_splits("odd_out")
                    layer_norm(2)
                    x_lo(3)

        @block.tensor
        def _(pe):
            def mm(out, lhs, rhs, start, stop):
                return nc.tensor.matmul(out, lhs, rhs, start=start, stop=stop)

            def turn_x(k, source):
                for g in range(8):
                    m, q = divmod(g, 4)
                    if g >= 2:
                        pe.wait_ge(sem(f"xt_lo{k}"), g - 1)
                    for c in range(4):
                        last = nc.tensor.transpose(
                            ps[:, 2 + g % 2, P * c:P * c + P],
                            source[:, m, (4 * q + c) * P:(4 * q + c + 1) * P], ident)
                    last.then_inc(sem(f"xt_ps{k}"), 1)
                pe.wait_ge(sem(f"xt_lo{k}"), 8)

            def feature(name):
                def one(b):
                    k = b.plus(first_block[name])
                    bank = ps[:, k.slot(2), :]
                    wait_round(pe, bank_free[k.slot(2)], k.turn(2))
                    for half in range(2):
                        g = b.times(2).plus(base[name] + half)
                        pe.wait_ge(lo_ready[g.slot(STAGES)], g.turn(STAGES, 1))
                        hi = w_hi[:, g.slot(SPLITS), :].rearrange("p (k n) -> p k n", k=8)
                        lo = w_lo[:, g.slot(SPLITS), :].rearrange("p (k n) -> p k n", k=8)
                        for c in range(8):
                            kc = 8 * half + c
                            both = xT[:, kc, :, :].rearrange("p s t -> p (s t)")
                            if kc < KC - 1:
                                mm(bank, hi[:, c, :], both, kc == 0, False)
                                last = mm(bank[:, 0:T], lo[:, c, :], xT[:, kc, 0, :], False, False)
                            else:
                                mm(bank[:, 0:T], lo[:, c, :], xT[:, kc, 0, :], False, False)
                                last = mm(bank, hi[:, c, :], both, False, True)
                        last.then_inc(used[g.slot(SPLITS)], 1)

                repeat(pe, 0, n_blocks(name), 2, one, peel=0 if first_block[name] else 2)

            def token_unit(g, lhs, banks, start, stop, done=None):
                pe.wait_ge(lo_ready[g.slot(STAGES)], g.turn(STAGES, 1))
                hi, lo = w_hi[:, g.slot(SPLITS), :], w_lo[:, g.slot(SPLITS), :]
                for m in range(2):
                    xh, xl = (lhs[:, s, m * P:(m + 1) * P] for s in range(2))
                    out = [ps[:, banks[m] + c, :] for c in range(2)]
                    for c in range(2):
                        mm(out[c], xh, hi[:, 512 * c:512 * c + 512], start, False)
                    for c in range(2):
                        mm(out[c], xh, lo[:, 512 * c:512 * c + 512], False, False)
                    for c in range(2):
                        last = mm(out[c], xl, hi[:, 512 * c:512 * c + 512], False, stop)
                last.then_inc(used[g.slot(SPLITS)], 1)

            def token(name, halves, first_bank):
                for kc in range(KC):
                    for half in range(halves):
                        g = At(base[name] + halves * kc + half)
                        banks = [first_bank + 2 * halves * m + 2 * half for m in range(2)]
                        token_unit(g, xT[:, kc, :, :], banks, kc == 0, kc == KC - 1)

            def token_done(name, done, n=1):
                g = At(base[name] + t[name].shape[0] - 1)
                pe.wait_ge(used[g.slot(SPLITS)], g.turn(SPLITS, 1))
                pe.sem_inc(sem(done), n)

            def latent():
                pe.wait_ge(sem("sq"), 1)
                for k in range(4):
                    mm(ps[:, 2, 0:T], ones, squares[:, T * k:T * k + T], k == 0, k == 3)
                for k in range(2):
                    last = mm(ps[:, 2, T:2 * T], ones, squares[:, T * (4 + k):T * (5 + k)], k == 0,
                              k == 1)
                last.then_inc(sem("sq_ps"), 1)
                pe.wait_ge(sem("latents"), 1)
                for n in range(14):
                    if n >= 2:
                        pe.wait_ge(sem("mla_out"), n - 1)
                    bank = ps[:, 2 + n % 2, :]
                    if n < 10:
                        w, kc, at = (w_qb, 4, CQN) if n < 6 else (w_kvb, 2, CKVN)
                        for j in range(2):
                            col = P * (2 * (n if n < 6 else n - 6) + j)
                            for k in range(kc):
                                last = mm(bank[:, T * j:T * j + T], w[:, k, col:col + P],
                                          arena[:, at + k, :], k == 0, k == kc - 1)
                    else:
                        m, c = divmod(n - 10, 2)
                        for k in range(2):
                            last = mm(bank, arena[:, CKVN + k, m * P:(m + 1) * P],
                                      w_kvb[:, k, 1024 + 512 * c:1536 + 512 * c], k == 0, k == 1)
                    last.then_inc(sem("mla_ps"), 1)

            def rotate(n, at, count, rot):
                if n >= 2:
                    pe.wait_ge(sem("roped"), n - 1)
                mm(ps[:, 4 + n % 2, 0:count * T], rot, blocks(at, count), True, True).then_inc(
                    sem("rot_ps"), 1)

            def logits(h):
                bank = ps[:, 2 + h % 2, :]
                if h >= 2:
                    pe.wait_ge(sem("max_ready"), h - 1)
                if h < HEADS:
                    parts = [(arena[:, Q_AT + h, :], arena[:, K_AT + h, :])]
                else:
                    j = h - HEADS
                    half = slice(ROPE * (j % 2), ROPE * (j % 2) + ROPE)
                    parts = [(arena[:, QB + j, :], arena[:, KN + j, :]),
                             (arena[half, QB + 8 + j // 2, :], arena[half, KR_AT, :])]
                for m in range(2):
                    out = bank[:, 128 * m:128 + 256 * m]
                    for n, (q, k) in enumerate(parts):
                        last = mm(out, q[:, m * P:(m + 1) * P], k[:, 0:P * (m + 1)], n == 0,
                                  n == len(parts) - 1)
                last.then_inc(sem("logit_ps"), 1)

            def turn_probs(h):
                pe.wait_ge(sem("probs_ready"), h + 1)
                if h >= 2:
                    pe.wait_ge(sem("turned"), h - 1)
                for b in range(3):
                    last = nc.tensor.transpose(ps[:, 4 + h % 2, P * b:P * b + P],
                                               probs[:, h % 2, P * b:P * b + P], ident)
                last.then_inc(sem("turned_ps"), 1)

            def head(layer, h, weights, ready, val, col):
                pe.wait_ge(sem(ready), h + 1)
                if h >= 2:
                    pe.wait_ge(sem(f"heads_lo{layer}"), h - 1)
                bank = ps[:, 6 + h % 2, :]
                mm(bank[:, 0:T], val[:, 0, col:col + P], weights[:, h % 2, 0:T], True, False)
                mm(bank[:, P:T], val[:, 1, col:col + P], weights[:, h % 2, T:384], False,
                   True).then_inc(sem(f"head_ps{layer}"), 1)

            def head_even(h):
                head(0, h, probs_t, "turned", val_a if h < HEADS else val_b, P * (h % HEADS))

            def stick_z(h):
                if h >= 2:
                    pe.wait_ge(sem("zmax_ready"), h - 1)
                bank = ps[:, 2 + h % 2, :]
                q, k = arena[:, OQ_AT + h, :], arena[:, OK_AT + h, :]
                mm(bank[:, 0:T], k[:, 0:P], q, True, True)
                mm(bank[:, T:384], k[:, P:T], q[:, P:T], True, True).then_inc(sem("z_ps"), 1)

            def stick_suffix(h):
                pe.wait_ge(sem("rest_ready"), h + 1)
                if h >= 2:
                    pe.wait_ge(sem("att_ready"), h - 1)
                bank, rest = ps[:, 4 + h % 2, :], log_rest[:, h % 2, :]
                q, k = arena[:, OQ_AT + h, :], arena[:, OK_AT + h, :]
                mm(bank[:, 0:T], tri, rest[:, 0:T], True, False)
                mm(bank[:, P:T], ones, rest[:, T:384], False, False)
                mm(bank[:, 0:P], ident, diag_mask, False, False)
                mm(bank[:, 0:T], k[:, 0:P], q, False, True)
                mm(bank[:, T:384], tri, rest[:, T:384], True, False)
                mm(bank[:, T:384], ident, diag_mask, False, False)
                mm(bank[:, T:384], k[:, P:T], q[:, P:T], False, True).then_inc(sem("suffix_ps"), 1)

            def retrieve(layer):
                pe.wait_ge(sem(f"keys_in{layer}"), 16)
                for m in range(2):
                    for g in range(4):
                        n = 4 * m + g
                        if n >= 2:
                            pe.wait_ge(sem(f"scores{layer}"), n - 1)
                        for j in range(4):
                            s = 4 * g + j
                            last = mm(ps[:, 2 + n % 2, P * j:P * j + P],
                                      arena[:, QT_AT + s, m * P:(m + 1) * P], keys_t[:, s, :],
                                      True, True)
                        last.then_inc(sem(f"score_ps{layer}"), 1)
                    pe.wait_ge(sem(f"picks_done{layer}"), m + 1)
                    if m:
                        pe.wait_ge(sem(f"picks_T{layer}"), 1)
                    for w in range(3):
                        last = nc.tensor.transpose(ps[:, 4, P * w:P * w + P], picked[:, w, :], ident)
                    last.then_inc(sem(f"picks_ps{layer}"), 1)

            def gate(layer):
                def group(g):
                    wait_round(pe, sem(f"group{layer}_{g.slot(2)}"), g.turn(2))
                    for r in range(2):
                        pe.wait_ge(sem(f"hots{layer}_{r}"), g.turn(1, 1))
                        for j in range(2):
                            col = P * (2 * r + j)
                            last = mm(ps[:, 2 + g.slot(2), col:col + P], onehot[:, r, j, 0, :],
                                      onehot[:, r, j, 1, :], True, True)
                        last.then_inc(sem(f"pair_ps{layer}_{r}"), 1)

                repeat(pe, 0, T // 4, 2, group, peel=2)

            def values(layer):
                name = f"v{layer}"

                def row(b, start=False, stop=False):
                    pe.wait_ge(sem(f"h_lo{layer}"), b.turn(1, 1))
                    for half in range(2):
                        token_unit(b.times(2).plus(base[name] + half), xT[:, b.slot(2), :, :],
                                   [2 * half, 4 + 2 * half], start, stop)

                for s in range(2):
                    pe.wait_ge(sem(f"group{layer}_{s}"), T // 8)
                row(At(0), start=True)
                row(At(1))
                repeat(pe, 2, P - 2, 2, row)
                row(At(P - 2))
                row(At(P - 1), stop=True)

            pe.wait_ge(sem("const_in"), 16)
            pe.wait_ge(sem("x_in"), 16)
            turn_x(0, x_first)
            feature("even_in")
            token("even_v", 1, 4)
            token_done("even_v", "va_ps")
            latent()
            pe.wait_ge(sem("mla_out"), 14)
            for n in range(8):
                rotate(n, Q_AT + 2 * n, 2, rot_a)
            rotate(8, KR_AT, 1, rot_b)
            for n in range(2):
                rotate(9 + n, QB + 8 + 2 * n, 2, rot_b)
            pe.wait_ge(sem("roped"), 11)
            pe.wait_ge(sem("va_out"), 1)
            logits(0)
            for h in range(2 * HEADS):
                if h + 1 < 2 * HEADS:
                    logits(h + 1)
                turn_probs(h)
                if h:
                    head_even(h - 1)
            head_even(2 * HEADS - 1)
            pe.wait_ge(sem("heads_lo0"), 16)
            token("even_out", 2, 0)
            token_done("even_out", "y_ps0", 8)
            pe.wait_ge(sem("ln_done0"), 1)
            turn_x(1, residual)
            for layer in range(2):
                feature(f"query{layer}")
                pe.wait_ge(bank_free[0], (first_block[f"query{layer}"] + 16 + 1) // 2)
                pe.wait_ge(bank_free[1], (first_block[f"query{layer}"] + 16) // 2)
                pe.sem_inc(sem(f"qT_ready{layer}"), 1)
                retrieve(layer)
                feature(f"u{layer}")
                gate(layer)
                values(layer)
                token_done(f"v{layer}", f"y_ps{2 * layer + 1}", 8)
                if layer == 0:
                    pe.sem_inc(sem("pe_v_done0"), 1)
                    pe.wait_ge(sem("ln_done1"), 1)
                    turn_x(2, residual)
                    feature("odd_in")
                    pe.wait_ge(bank_free[0], (first_block["odd_in"] + 32 + 1) // 2)
                    pe.wait_ge(bank_free[1], (first_block["odd_in"] + 32) // 2)
                    token("odd_v", 2, 0)
                    token_done("odd_v", "vc_ps")
                    pe.wait_ge(sem("vc_out"), 1)
                    pe.wait_ge(sem("q_scaled"), 1)
                    pe.wait_ge(sem("odd_in"), 16)
                    stick_z(0)
                    for h in range(C_HEADS):
                        if h + 1 < C_HEADS:
                            stick_z(h + 1)
                        stick_suffix(h)
                        if h:
                            head(1, h - 1, att, "att_ready", val_c, P * (h - 1))
                    head(1, C_HEADS - 1, att, "att_ready", val_c, P * (C_HEADS - 1))
                    pe.wait_ge(sem("heads_lo1"), 16)
                    token("odd_out", 2, 0)
                    token_done("odd_out", "y_ps2", 8)
                    pe.wait_ge(sem("ln_done2"), 1)
                    turn_x(3, residual)


def feature_units(w):
    n = w.shape[1] // P
    return np.ascontiguousarray(
        w.reshape(2, 8, P, n, P).transpose(3, 0, 2, 1, 4).reshape(2 * n, P, UNIT))


def token_units(w):
    n = w.shape[1] // UNIT
    return np.ascontiguousarray(w.reshape(KC, P, n, UNIT).transpose(0, 2, 1, 3).reshape(KC * n, P, UNIT))


def shape_constants():
    eye = np.eye(P, dtype=np.float32)
    iota = np.tile(np.arange(P, dtype=np.float32), (P, 1))
    ones = np.ones((P, P), np.float32)

    def rotation(half):
        r = np.zeros((P, P), np.float32)
        for m in range(P):
            low = m % (2 * half) < half
            r[m + half if low else m - half, m] = -1.0 if low else 1.0
        return r

    const = np.stack([eye, ones, iota, rotation(64), rotation(32)], 1)

    def angles(half):
        inv = np.float32(10000.0) ** (-np.arange(half, dtype=np.float32) / np.float32(half))
        ang = (np.arange(T, dtype=np.float32)[:, None] * inv[None, :]).astype(np.float32).T
        ang = np.tile(ang, (P // half, 1))
        return np.cos(ang).astype(np.float32), np.sin(ang).astype(np.float32)

    trig = np.stack([*angles(64), *angles(32)], 1)
    q, k = np.arange(T)[:, None], np.arange(T)[None, :]
    back = q - k
    count = (((back >= 0) & (back <= 128)).astype(np.float32) + ((back >= 0) & (back % 4 == 0))
             + ((back >= 0) & (back % 16 == 0)))

    def tiles(a):
        return np.concatenate([a[0:P, 0:P], a[P:T, 0:T]], 1)

    even_masks = np.stack([tiles(count), tiles(np.where(count > 0, 0.0, NEG)),
                           tiles(np.where(back >= 0, 0.0, NEG))], 1).astype(np.float32)
    j, s = np.arange(P)[:, None], np.arange(P)[None, :]
    tri = (j >= s).astype(np.float32)
    earlier = (j < s)
    diag = np.where(earlier, 0.0, NEG).astype(np.float32)
    neg = -np.concatenate([earlier, np.ones((P, P)), earlier], 1).astype(np.float32)
    odd_consts = np.concatenate([tri, diag, neg], 1).astype(np.float32)
    return {"const": const, "trig": trig, "even_masks": even_masks, "odd_consts": odd_consts}


def layout(i):
    i = {k: np.asarray(v) for k, v in i.items()}
    w = i["a_w_in"][0]
    a, cq, ckv = 1024, 3072, 3584
    kr = w[:, 3840:3904]
    feats = np.concatenate([w[:, 0:2 * a], w[:, cq:ckv], w[:, ckv:3840], kr, kr], 1)
    wq = i["b_w_q_b"][0].reshape(4, P, HEADS, 192)
    wq = np.concatenate([wq[..., 0:P].reshape(4, P, 1024), wq[..., P:].reshape(4, P, 512)], 2)
    wkv = i["b_w_kv_b"][0].reshape(2, P, HEADS, 256)
    wkv = np.concatenate([wkv[..., 0:P].reshape(2, P, 1024), wkv[..., P:].reshape(2, P, 1024)], 2)
    c = np.ascontiguousarray
    t = {
        "x": c(i["x"].reshape(T, D)),
        "even_in": feature_units(feats), "even_v": token_units(w[:, 2 * a:3 * a]),
        "even_out": token_units(i["ab_w_out"][0]),
        "odd_in": feature_units(i["c_w_in"][0][:, 0:4096]),
        "odd_v": token_units(i["c_w_in"][0][:, 4096:]),
        "odd_out": token_units(i["c_w_out"][0]),
        "w_qb": c(wq.transpose(1, 0, 2)), "w_kvb": c(wkv.transpose(1, 0, 2)),
        "q_gain": c(i["b_q_norm"][0].reshape(4, P).T), "kv_gain": c(i["b_kv_norm"][0].reshape(2, P).T),
        "keys_t": c(i["peer_sub_keys"].reshape(2, 16, N_KEYS, P).transpose(0, 3, 1, 2)),
        "ln_gain": c(i["ln_gain"].reshape(4, D)), "ln_bias": c(i["ln_bias"].reshape(4, D)),
    }
    for n in range(2):
        t[f"query{n}"] = feature_units(i["peer_w_query"][n])
        u = i["peer_u"][n].reshape(P, P, 2, 8, P)
        t[f"u{n}"] = c(u.transpose(1, 2, 4, 3, 0)).reshape(2 * P, P, UNIT)
        v = i["peer_v"][n].reshape(P, P, 2, UNIT)
        t[f"v{n}"] = c(v.transpose(1, 2, 0, 3)).reshape(2 * P, P, UNIT)
    t.update(shape_constants())
    return t


def kernel(**inputs):
    import concourse.bacc as bacc
    from concourse.bass_utils import run_bass_kernel_spmd

    nc = bacc.Bacc("TRN2", target_bir_lowering=False, num_devices=1)
    arrays = layout(inputs)
    t = {}
    for name, a in arrays.items():
        t[name] = nc.dram_tensor(f"in_{name}", a.shape, mybir.dt.from_np(a.dtype),
                                 kind="ExternalInput").ap()
    t["kept"] = nc.dram_tensor("kept", (3, T, D), F32).ap()
    t["out"] = nc.dram_tensor("out_x", (T, D), F32, kind="ExternalOutput").ap()
    decoder(nc, t)
    r = run_bass_kernel_spmd(nc, [{f"in_{name}": a for name, a in arrays.items()}], core_ids=[0])
    return r.results[0]["out_x"].reshape(1, T, D)
```

```python
from contextlib import ExitStack

import concourse.bass as bass
import concourse.mybir as mybir
import numpy as np
from concourse.alu_op_type import AluOpType as ALU

ACT = mybir.ActivationFunctionType
AX = mybir.AxisListType
F32 = mybir.dt.float32
F32R = mybir.dt.float32r
U32 = mybir.dt.uint32

P = 128
D = 2048
T = 256
TILES = T // P
KC = D // P
UNIT = 1024
STAGES = 4
HALF = UNIT // 2
SPLITS = 4
HEADS = 8
C_HEADS = 16
TOPK = 16
N_KEYS = 128
Q_LORA = 512
KV_LORA = 256
ROPE = 64
ALPHA = float(4 ** 0.25)
LN_EPS = 1e-5
RMS_EPS = 1e-6
NEG = -1e30
REPLACED = -3.0e38
A_SCALE = float(128 ** -0.5)
B_SCALE = float((128 + 64) ** -0.5)

PICK_END = 48
CUT = 80
GROUP = 4
GROUPS = T // GROUP
GATE_STEP = 38
PICK_PARTS = 46
LATE_CHUNK = 6
LATE_CHUNKS = (P - CUT) // LATE_CHUNK
LATE_GROUPS = GROUPS // LATE_CHUNKS


class At:

    def __init__(self, c, i=None, step=0):
        self.c, self.i, self.step = c, i, step

    def plus(self, n):
        return At(self.c + n, self.i, self.step)

    def times(self, n):
        return At(self.c * n, self.i, self.step * n)

    def index(self):
        return self.c if self.i is None else self.i * self.step + self.c

    def slot(self, ring):
        return self.c % ring

    def turn(self, ring, more=0, each=1):
        c = (self.c // ring + more) * each
        return c if self.i is None else self.i * (self.step // ring * each) + c


def repeat(eng, first, last, step, body, peel=0):
    for c in range(first, first + peel):
        body(At(c))
    first += peel
    n = (last - first) // step
    if n >= 2:
        with eng.Fori(0, n) as i:
            for r in range(step):
                body(At(first + r, i, step))
        first += n * step
    for c in range(first, last):
        body(At(c))


def wait_round(eng, s, turns):
    if not isinstance(turns, int) or turns > 0:
        eng.wait_ge(s, turns)


def decoder(nc, t):
    with ExitStack() as ctx:
        def sb(name, shape, dt=F32):
            return ctx.enter_context(nc.sbuf_tensor(name, shape, dt))

        sems = {}

        def sem(name):
            if name not in sems:
                sems[name] = ctx.enter_context(nc.semaphore(name))
            return sems[name]

        arena = sb("arena", [P, P, T])
        xT = sb("xT", [P, KC, 2, T], F32R)
        stage = sb("stage", [P, STAGES, UNIT])
        w_hi = sb("w_hi", [P, SPLITS, HALF], F32R)
        w_lo = sb("w_lo", [P, SPLITS, HALF], F32R)
        half_sum = sb("half_sum", [P, 2, T])
        const = sb("const", [P, 3, P])
        picks = sb("picks", [P, 3, T])
        hot1 = sb("hot1", [P, 2, GROUP, P])
        hot2 = sb("hot2", [P, 2, GROUP * CUT])
        small = sb("small", [P, 224])
        ps = ctx.enter_context(nc.psum_tensor("ps", [P, 8, 512], F32))

        ident, ones, iota = (const[:, k, :] for k in range(3))
        q_gain, kv_gain = small[:, 0:4], small[:, 4:6]
        mean_var = small[:, 8:12].rearrange("p (m k) -> p m k", m=2)
        rstd = small[:, 12:14]
        bn = small[:, 16:64].rearrange("p (m c k) -> p m c k", m=2, c=4)
        neg_max = small[:, 64:96].rearrange("p (h m) -> p h m", m=2)
        row_sum = small[:, 96:128].rearrange("p (h m) -> p h m", m=2)
        inv_sum = small[:, 128:160].rearrange("p (h m) -> p h m", m=2)
        gate_sum = small[:, 160:176].rearrange("p (m h) -> p m h", m=2)
        gate_inv = small[:, 176:192].rearrange("p (m h) -> p m h", m=2)
        ln_eps, rms_eps = small[:, 192:193], small[:, 193:194]

        def blocks(first, count):
            return arena[:, first:first + count, :].rearrange("p b t -> p (b t)")

        residual = blocks(0, 16).rearrange("p (m d) -> p m d", m=2)
        gain, bias = blocks(16, 8), blocks(24, 8)
        RAW, Q_AT, K_AT, CQ_AT, CKV_AT, KR_AT = 0, 0, 8, 16, 20, 22
        val_a = blocks(23, 8).rearrange("p (m d) -> p m d", m=2)
        x_first = blocks(31, 16).rearrange("p (m d) -> p m d", m=2)
        CQN, CKVN, QB, KN = 31, 35, 37, 49
        val_b = blocks(57, 8).rearrange("p (m d) -> p m d", m=2)
        w_qb = blocks(65, 24).rearrange("p (k n) -> p k n", k=4)
        w_kvb = blocks(89, 16).rearrange("p (k n) -> p k n", k=2)
        even_masks = blocks(105, 5)[:, 0:1152].rearrange("p (k n) -> p k n", k=3)
        trig = arena[:, 110:114, :]
        rot_a, rot_b = hot1[:, 0, 0, :], hot1[:, 0, 1, :]
        probs = blocks(114, 3).rearrange("p (r n) -> p r n", r=2)
        probs_t = blocks(117, 3).rearrange("p (r n) -> p r n", r=2)
        squares = blocks(120, 6)
        rms = arena[:, 126:128, :]
        rotated = blocks(120, 4).rearrange("p (r n) -> p r n", r=2)
        OQ_AT, OK_AT = 0, 16
        val_c = blocks(32, 16).rearrange("p (m d) -> p m d", m=2)
        odd_consts = blocks(48, 3)
        tri, diag_mask, neg_mask = odd_consts[:, 0:128], odd_consts[:, 128:256], odd_consts[:, 256:640]

        def ring2(first):
            return blocks(first, 3).rearrange("p (r n) -> p r n", r=2)

        z_abs, z_exp, z_log, z_max, log_rest, att = (ring2(51 + 3 * k) for k in range(6))
        QT_AT = 48
        keys_t = blocks(64, 8).rearrange("p (s n) -> p s n", s=16)
        scores = blocks(72, 16).rearrange("p (s n) -> p s n", s=32)
        scores_cut = blocks(88, 16).rearrange("p (s n) -> p s n", s=32)
        top_v = blocks(104, 2).rearrange("p (s k) -> p s k", s=32)
        top_i = blocks(106, 2).bitcast(U32).rearrange("p (s k) -> p s k", s=32)
        top_f = blocks(108, 2)
        cand = blocks(110, 16).rearrange("p (s n) -> p s n", s=16)
        cand_cut = blocks(48, 16).rearrange("p (s n) -> p s n", s=16)
        best_v = blocks(126, 1).rearrange("p (s k) -> p s k", s=16)
        best_i = blocks(127, 1).bitcast(U32)
        rank_i = blocks(64, 2).bitcast(U32).rearrange("p (s n) -> p s n", s=2)
        rank_f = blocks(66, 2).rearrange("p (s m n) -> p s m n", s=2, m=2)
        picked = blocks(68, 3).rearrange("p (m w n) -> p m w n", m=2, w=3)
        shifted = blocks(71, 1).rearrange("p (m h k) -> p m h k", m=2, h=HEADS)
        match = blocks(72, 8)
        by_group = arena[:, :, :].rearrange("p i (g t) -> p i g t", t=GROUP)

        order = [("even_in", "even_in"), ("even_v", "even_v"), ("even_out", "even_out"),
                 ("query0", "query0"), ("u0", "u0"), ("v0", "v0"),
                 ("odd_in", "odd_in"), ("odd_v", "odd_v"), ("odd_out", "odd_out"),
                 ("query1", "query1"), ("u1", "u1"), ("v1", "v1")]
        base, at = {}, 0
        for name, _ in order:
            base[name] = at
            at += t[name].shape[0]
        FEATURE = ["even_in", "query0", "u0", "odd_in", "query1", "u1"]
        first_block, at = {}, 0
        for name in FEATURE:
            first_block[name] = at
            at += t[name].shape[0] // 2

        def n_blocks(name):
            return t[name].shape[0] // 2

        staged = [sem(f"staged{s}") for s in range(STAGES)]
        hi_ready = [sem(f"hi_ready{s}") for s in range(SPLITS)]
        lo_ready = [sem(f"lo_ready{s}") for s in range(SPLITS)]
        used = [sem(f"used{s}") for s in range(SPLITS)]
        half_ready = [sem(f"half_ready{s}") for s in range(2)]
        bank_free = [sem(f"bank_free{s}") for s in range(2)]
        half_free = [sem(f"half_free{s}") for s in range(2)]
        hots_ready = [sem(f"hots_ready{s}") for s in range(2)]
        group_ps = [sem(f"group_ps{s}") for s in range(2)]
        group_out = [sem(f"group_out{s}") for s in range(2)]

        def group_at(layer, late, g):
            return g.plus(GROUPS * (2 * layer + late))

        block = ctx.enter_context(nc.Block())

        @block.sync
        def _(sp):
            for name, _ in order:
                units = t[name]

                def load(a, units=units, name=name):
                    g = a.plus(base[name])
                    second = g.times(2).plus(1)
                    wait_round(sp, lo_ready[second.slot(SPLITS)],
                               second.turn(SPLITS, 1 - 2 * STAGES // SPLITS))
                    sp.dma_start(stage[:, g.slot(STAGES), :], units[a.index()]).then_inc(
                        staged[g.slot(STAGES)], 16)

                repeat(sp, 0, units.shape[0], STAGES, load, peel=0 if base[name] else STAGES)

        @block.gpsimd
        def _(pool):
            def get(dst, src, s):
                pool.dma_start(dst, src).then_inc(sem(s), 16)

            get(x_first, t["x"].rearrange("(m p) d -> p m d", p=P), "x_in")
            get(const[:, :, :], t["const"], "const_in")
            get(q_gain, t["q_gain"], "mla_in")
            get(kv_gain, t["kv_gain"], "mla_in")
            get(w_qb, t["w_qb"], "mla_in")
            get(w_kvb, t["w_kvb"], "mla_in")
            get(even_masks, t["even_masks"], "mla_in")
            get(trig, t["trig"], "mla_in")
            get(hot1[:, 0, 0:2, :], t["rotations"], "mla_in")

            def norm_in(k, source):
                get(residual, source, f"ln_in{k}")
                get(gain, t["ln_gain"][k].partition_broadcast(P), f"ln_in{k}")
                get(bias, t["ln_bias"][k].partition_broadcast(P), f"ln_in{k}")

            def keep(k):
                pool.wait_ge(sem(f"ln_done{k}"), 1)
                get(t["kept"][k].rearrange("(m p) d -> p m d", p=P), residual, f"kept{k}")
                pool.wait_ge(sem(f"kept{k}"), 16)

            pool.wait_ge(sem("heads_lo0"), 16)
            norm_in(0, t["x"].rearrange("(m p) d -> p m d", p=P))
            for layer in range(2):
                keep(2 * layer)
                pool.wait_ge(sem(f"qT_ready{layer}"), 1)
                get(keys_t, t["keys_t"][layer], f"keys_in{layer}")
                pool.wait_ge(sem(f"h_lo{layer}"), 33)
                norm_in(2 * layer + 1, t["kept"][2 * layer].rearrange("(m p) d -> p m d", p=P))
                if layer == 0:
                    keep(1)
                    pool.wait_ge(sem("pe_v_done0"), 1)
                    get(odd_consts[:, 0:640], t["odd_consts"], "odd_in")
                    pool.wait_ge(sem("heads_lo1"), 16)
                    norm_in(2, t["kept"][1].rearrange("(m p) d -> p m d", p=P))
            pool.wait_ge(sem("ln_done3"), 1)
            get(t["out"].rearrange("(m p) d -> p m d", p=P), residual, "out_done")
            pool.wait_ge(sem("out_done"), 16)

        @block.scalar
        def _(act):
            def split_hi(g):
                act.wait_ge(staged[g.slot(STAGES)], g.turn(STAGES, 1, 16))
                for q in range(2):
                    h = g.times(2).plus(q)
                    wait_round(act, used[h.slot(SPLITS)], h.turn(SPLITS))
                    nc.scalar.activation(w_hi[:, h.slot(SPLITS), :],
                                         stage[:, g.slot(STAGES), HALF * q:HALF * q + HALF],
                                         ACT.Copy).then_inc(hi_ready[h.slot(SPLITS)], 1)

            def token_splits(name):
                repeat(act, base[name], base[name] + t[name].shape[0], STAGES, split_hi)

            def copy_half(name, b):
                last = b.times(4).plus(2 * base[name] + 3)
                act.wait_ge(used[last.slot(SPLITS)], last.turn(SPLITS, 1))
                k = b.plus(first_block[name])
                nc.scalar.activation(half_sum[:, k.slot(2), :], ps[:, k.slot(2), T:2 * T],
                                     ACT.Copy).then_inc(half_ready[k.slot(2)], 1)

            def feature(name):
                def splits(b):
                    split_hi(b.times(2).plus(base[name]))
                    split_hi(b.times(2).plus(base[name] + 1))

                def step(b):
                    splits(b)
                    copy_half(name, b.plus(-1))

                splits(At(0))
                repeat(act, 1, n_blocks(name), 2, step)
                copy_half(name, At(n_blocks(name) - 1))

            def experts(layer):
                name = f"u{layer}"

                def splits(b):
                    split_hi(b.times(2).plus(base[name]))
                    split_hi(b.times(2).plus(base[name] + 1))

                def wait_added(b):
                    k = b.plus(first_block[name])
                    act.wait_ge(bank_free[k.slot(2)], k.turn(2, 1))

                def gelu(b):
                    nc.scalar.activation(arena[:, b.index(), :], arena[:, b.index(), :],
                                         ACT.Gelu).then_inc(sem(f"gelu{layer}"), 1)

                def early(b):
                    splits(b)
                    wait_added(b.plus(-2))
                    copy_half(name, b.plus(-1))
                    gelu(b.plus(-2))

                def c_out(g):
                    k = group_at(layer, 0, g)
                    c = ps[:, 2 + k.slot(2), 0:GROUP * (P - CUT)].rearrange(
                        "p (t i) -> p i t", t=GROUP)
                    nc.scalar.activation(by_group[:, CUT:P, g.index(), :], c, ACT.Copy).then_inc(
                        group_out[k.slot(2)], 1)

                def building(n):
                    for r in range(2):
                        b = n.times(2).plus(PICK_END + r)
                        splits(b)
                        wait_added(b.plus(-2))
                        before = [n.times(4).plus(2 * r - 2 + j) for j in range(2)]
                        first = n.i is None and n.c == 0 and r == 0
                        if not first:
                            for g in before:
                                k = group_at(layer, 0, g)
                                act.wait_ge(group_ps[k.slot(2)], k.turn(2, 1))
                        copy_half(name, b.plus(-1))
                        gelu(b.plus(-2))
                        if not first:
                            for g in before:
                                c_out(g)

                def late_gelu(b):
                    k = b.plus(first_block[name])
                    wait_added(b)
                    nc.scalar.activation(half_sum[:, k.slot(2), :], half_sum[:, k.slot(2), :],
                                         ACT.Gelu).then_inc(sem(f"late_gelu{layer}"), 1)

                def late_half(b):
                    if not (b.i is None and b.c < CUT + 2):
                        before = b.plus(-CUT + layer * (P - CUT))
                        act.wait_ge(half_free[before.slot(2)], before.turn(2))
                    copy_half(name, b)

                def late(n):
                    for r in range(LATE_CHUNK):
                        b = n.times(LATE_CHUNK).plus(CUT + r)
                        splits(b)
                        if n.i is None and n.c == 0 and r < 2:
                            wait_added(b.plus(-2))
                            if r == 0:
                                for g in (GROUPS - 2, GROUPS - 1):
                                    k = group_at(layer, 0, At(g))
                                    act.wait_ge(group_ps[k.slot(2)], k.turn(2, 1))
                                copy_half(name, b.plus(-1))
                            else:
                                late_half(b.plus(-1))
                            gelu(b.plus(-2))
                            if r == 0:
                                for g in (GROUPS - 2, GROUPS - 1):
                                    c_out(At(g))
                        else:
                            late_half(b.plus(-1))
                            late_gelu(b.plus(-2))

                splits(At(0))
                splits(At(1))
                copy_half(name, At(0))
                nc.scalar.preload_act_table(ACT.Gelu)
                repeat(act, 2, GATE_STEP, 2, early)
                act.wait_ge(sem(f"shifted{layer}"), 1)
                for m in range(2):
                    for h in range(HEADS):
                        last = nc.scalar.activation(picked[:, m, 2, TOPK * h:TOPK * h + TOPK],
                                                    shifted[:, m, h, :], ACT.Exp,
                                                    accum_out=gate_sum[:, m, h:h + 1])
                last.then_inc(sem(f"gate_exp{layer}"), 1)
                nc.scalar.preload_act_table(ACT.Gelu)
                repeat(act, GATE_STEP, PICK_END, 2, early)
                act.wait_ge(sem(f"picks_ps{layer}"), 1)
                for m in range(2):
                    last = nc.scalar.activation(
                        picks[:, :, m * P:(m + 1) * P],
                        ps[:, 2 + m, 0:384].rearrange("p (w t) -> p w t", w=3), ACT.Copy)
                last.then_inc(sem(f"picks_T{layer}"), 1)
                repeat(act, 0, GROUPS // 4, 1, building, peel=1)
                repeat(act, 0, LATE_CHUNKS, 1, late, peel=1)
                late_half(At(P - 1))
                late_gelu(At(P - 2))
                late_gelu(At(P - 1))

            def x_hi(k):
                for g in range(8):
                    m, q = divmod(g, 4)
                    act.wait_ge(sem(f"xt_ps{k}"), g + 1)
                    nc.scalar.activation(
                        xT[:, 4 * q:4 * q + 4, 0, m * P:(m + 1) * P],
                        ps[:, 2 + g % 2, :].rearrange("p (c t) -> p c t", c=4),
                        ACT.Copy).then_inc(sem(f"xt_hi{k}"), 1)

            def ln_std(k):
                act.wait_ge(sem(f"ln_stats{k}"), 1)
                nc.scalar.activation(rstd, mean_var[:, :, 1], ACT.Sqrt, bias=ln_eps).then_inc(
                    sem(f"ln_std{k}"), 1)

            def latent():
                b22 = first_block["even_in"] + n_blocks("even_in") - 1
                act.wait_ge(bank_free[b22 % 2], b22 // 2 + 1)
                act.wait_ge(bank_free[(b22 - 1) % 2], (b22 - 1) // 2 + 1)
                nc.scalar.activation(squares, blocks(CQ_AT, 6), ACT.Square).then_inc(sem("sq"), 1)
                act.wait_ge(sem("sq_ps"), 1)
                act.wait_ge(sem("eps_set"), 1)
                nc.scalar.activation(rms[:, 0, :], ps[:, 2, 0:T], ACT.Sqrt, bias=rms_eps,
                                     scale=1.0 / Q_LORA)
                nc.scalar.activation(rms[:, 1, :], ps[:, 2, T:2 * T], ACT.Sqrt, bias=rms_eps,
                                     scale=1.0 / KV_LORA).then_inc(sem("rms_std"), 1)
                for n in range(14):
                    act.wait_ge(sem("mla_ps"), n + 1)
                    if n < 10:
                        dst = blocks((QB if n < 6 else KN - 12) + 2 * n, 2)
                    else:
                        m, c = divmod(n - 10, 2)
                        dst = val_b[:, m, 512 * c:512 * c + 512]
                    nc.scalar.activation(dst, ps[:, 2 + n % 2, :], ACT.Copy).then_inc(sem("mla_out"), 1)

            def soft_exp(h):
                act.wait_ge(sem("max_ready"), h + 1)
                for m in range(2):
                    e = probs[:, h % 2, 128 * m:128 + 256 * m]
                    kw = {"accum_out": row_sum[:, h, m:m + 1]} if h >= HEADS else {}
                    last = nc.scalar.activation(e, e, ACT.Exp, bias=neg_max[:, h, m:m + 1], **kw)
                last.then_inc(sem("exp_ready"), 1)

            def probs_out(h):
                act.wait_ge(sem("turned_ps"), h + 1)
                if h >= 2:
                    act.wait_ge(sem("head_ps0"), h - 1)
                nc.scalar.activation(probs_t[:, h % 2, :], ps[:, 4 + h % 2, 0:384],
                                     ACT.Copy).then_inc(sem("turned"), 1)

            def head_hi(layer, h):
                act.wait_ge(sem(f"head_ps{layer}"), h + 1)
                nc.scalar.activation(xT[:, h, 0, :], ps[:, 6 + h % 2, 0:T], ACT.Copy).then_inc(
                    sem(f"heads_hi{layer}"), 1)

            def stick_logs(h):
                r = h % 2
                act.wait_ge(sem("z_ps"), h + 1)
                nc.scalar.activation(z_abs[:, r, :], ps[:, 2 + r, 0:384], ACT.Abs).then_inc(
                    sem("abs_ready"), 1)
                act.wait_ge(sem("abs_ready"), h + 1)
                nc.scalar.activation(z_exp[:, r, :], z_abs[:, r, :], ACT.Exp, scale=-1.0).then_inc(
                    sem("zexp_ready"), 1)
                act.wait_ge(sem("zexp_ready"), h + 1)
                if h >= 2:
                    act.wait_ge(sem("rest_ready"), h - 1)
                nc.scalar.activation(z_log[:, r, :], z_exp[:, r, :], ACT.Ln, bias=1.0).then_inc(
                    sem("log_ready"), 1)

            def stick_att(h):
                act.wait_ge(sem("suffix_ps"), h + 1)
                if h >= 2:
                    act.wait_ge(sem("head_ps1"), h - 1)
                nc.scalar.activation(att[:, h % 2, :], ps[:, 4 + h % 2, 0:384], ACT.Exp).then_inc(
                    sem("att_ready"), 1)

            def scores_out(layer):
                for n in range(8):
                    act.wait_ge(sem(f"score_ps{layer}"), n + 1)
                    nc.scalar.activation(
                        scores[:, 4 * n:4 * n + 4, :].rearrange("p s n -> p (s n)"),
                        ps[:, 2 + n % 2, :], ACT.Copy).then_inc(sem(f"scores{layer}"), 1)

            def values(layer):
                name = f"v{layer}"

                def h_hi(b):
                    nc.scalar.activation(xT[:, b.slot(2), 0, :], arena[:, b.index(), :],
                                         ACT.Copy).then_inc(sem(f"h_hi{layer}"), 1)

                def row(b, more=True):
                    split_hi(b.times(2).plus(base[name]))
                    split_hi(b.times(2).plus(base[name] + 1))
                    if more:
                        h_hi(b.plus(1))

                for s in range(2):
                    act.wait_ge(group_out[s], GROUPS * (layer + 1))
                    act.wait_ge(half_free[s], (P - CUT) // 2 * (layer + 1))
                h_hi(At(0))
                repeat(act, 0, P - 2, 2, row)
                row(At(P - 2))
                row(At(P - 1), False)

            x_hi(0)
            feature("even_in")
            token_splits("even_v")
            for n in range(4):
                act.wait_ge(sem("va_ps"), 1)
                m, c = divmod(n, 2)
                last = nc.scalar.activation(val_a[:, m, 512 * c:512 * c + 512], ps[:, 4 + n, :],
                                            ACT.Copy)
            last.then_inc(sem("va_out"), 1)
            latent()
            soft_exp(0)
            for h in range(2 * HEADS):
                if h + 1 < 2 * HEADS:
                    soft_exp(h + 1)
                probs_out(h)
                if h:
                    head_hi(0, h - 1)
            head_hi(0, 2 * HEADS - 1)
            token_splits("even_out")
            ln_std(0)
            x_hi(1)
            for layer in range(2):
                feature(f"query{layer}")
                scores_out(layer)
                experts(layer)
                values(layer)
                ln_std(2 * layer + 1)
                if layer == 0:
                    x_hi(2)
                    feature("odd_in")
                    token_splits("odd_v")
                    for n in range(8):
                        act.wait_ge(sem("vc_ps"), 1)
                        m, c = divmod(n, 4)
                        last = nc.scalar.activation(val_c[:, m, 512 * c:512 * c + 512],
                                                    ps[:, n, :], ACT.Copy)
                    last.then_inc(sem("vc_out"), 1)
                    nc.scalar.preload_act_table_set("natural_log_exp_and_others")
                    stick_logs(0)
                    for h in range(C_HEADS):
                        if h + 1 < C_HEADS:
                            stick_logs(h + 1)
                        stick_att(h)
                        if h:
                            head_hi(1, h - 1)
                    head_hi(1, C_HEADS - 1)
                    token_splits("odd_out")
                    ln_std(2)
                    x_hi(3)

        @block.vector
        def _(dve):
            count = [0]

            def settle(ins):
                count[0] += 1
                ins.then_inc(sem("dve_steps"), 1)
                dve.wait_ge(sem("dve_steps"), count[0])

            def split_lo(g):
                for q in range(2):
                    h = g.times(2).plus(q)
                    dve.wait_ge(hi_ready[h.slot(SPLITS)], h.turn(SPLITS, 1))
                    nc.vector.tensor_tensor(w_lo[:, h.slot(SPLITS), :],
                                            stage[:, g.slot(STAGES), HALF * q:HALF * q + HALF],
                                            w_hi[:, h.slot(SPLITS), :].bitcast(F32),
                                            ALU.subtract).then_inc(lo_ready[h.slot(SPLITS)], 1)

            def token_splits(name):
                repeat(dve, base[name], base[name] + t[name].shape[0], STAGES, split_lo)

            def add_up(name, b, dest):
                k = b.plus(first_block[name])
                dve.wait_ge(half_ready[k.slot(2)], k.turn(2, 1))
                nc.vector.tensor_tensor(arena[:, b.plus(dest).index(), :], ps[:, k.slot(2), 0:T],
                                        half_sum[:, k.slot(2), :], ALU.add).then_inc(
                                            bank_free[k.slot(2)], 1)

            def feature(name, dest):
                n = n_blocks(name)

                def splits(b):
                    split_lo(b.times(2).plus(base[name]))
                    split_lo(b.times(2).plus(base[name] + 1))

                def step(b):
                    splits(b)
                    add_up(name, b.plus(-1), dest)

                splits(At(0))
                repeat(dve, 1, n, 2, step)
                add_up(name, At(n - 1), dest)

            def all_added(name):
                for b in (n_blocks(name) - 2, n_blocks(name) - 1):
                    k = At(b + first_block[name])
                    dve.wait_ge(bank_free[k.slot(2)], k.turn(2, 1))

            def x_lo(k):
                for g in range(8):
                    m, q = divmod(g, 4)
                    dve.wait_ge(sem(f"xt_hi{k}"), g + 1)
                    nc.vector.tensor_tensor(
                        xT[:, 4 * q:4 * q + 4, 1, m * P:(m + 1) * P],
                        ps[:, 2 + g % 2, :].rearrange("p (c t) -> p c t", c=4),
                        xT[:, 4 * q:4 * q + 4, 0, m * P:(m + 1) * P].bitcast(F32),
                        ALU.subtract).then_inc(sem(f"xt_lo{k}"), 1)

            def layer_norm(k):
                dve.wait_ge(sem(f"ln_in{k}"), 48)
                dve.wait_ge(sem(f"y_ps{k}"), 8)
                for m in range(2):
                    for c in range(4):
                        part = residual[:, m, 512 * c:512 * c + 512]
                        last = nc.vector.scalar_tensor_tensor(
                            out=part, in0=part, scalar=ALPHA, in1=ps[:, 4 * m + c, :],
                            op0=ALU.mult, op1=ALU.add)
                settle(last)
                for m in range(2):
                    for c in range(4):
                        last = nc.vector.bn_stats(bn[:, m, c, :],
                                                  residual[:, m, 512 * c:512 * c + 512])
                settle(last)
                for m in range(2):
                    last = nc.vector.bn_aggr(mean_var[:, m, :],
                                             bn[:, m, :, :].rearrange("p c k -> p (c k)"))
                last.then_inc(sem(f"ln_stats{k}"), 1)
                dve.wait_ge(sem(f"ln_std{k}"), 1)
                settle(nc.vector.reciprocal(rstd, rstd))
                for m in range(2):
                    last = nc.vector.tensor_scalar(residual[:, m, :], residual[:, m, :],
                                                   mean_var[:, m, 0:1], rstd[:, m:m + 1],
                                                   ALU.subtract, ALU.mult)
                settle(last)
                for m in range(2):
                    last = nc.vector.tensor_tensor(residual[:, m, :], residual[:, m, :], gain,
                                                   ALU.mult)
                settle(last)
                for m in range(2):
                    last = nc.vector.tensor_tensor(residual[:, m, :], residual[:, m, :], bias,
                                                   ALU.add)
                last.then_inc(sem(f"ln_done{k}"), 1)

            def latent():
                dve.wait_ge(sem("mla_in"), 16 * 7)
                dve.wait_ge(sem("rms_std"), 1)
                settle(nc.vector.reciprocal(rms, rms))
                for j in range(4):
                    nc.vector.scalar_tensor_tensor(
                        out=arena[:, CQN + j, :], in0=arena[:, CQ_AT + j, :],
                        scalar=q_gain[:, j:j + 1], in1=rms[:, 0, :], op0=ALU.mult, op1=ALU.mult)
                for j in range(2):
                    last = nc.vector.scalar_tensor_tensor(
                        out=arena[:, CKVN + j, :], in0=arena[:, CKV_AT + j, :],
                        scalar=kv_gain[:, j:j + 1], in1=rms[:, 1, :], op0=ALU.mult, op1=ALU.mult)
                last.then_inc(sem("latents"), 1)

            def rotate(n, at, count, which):
                x = arena[:, at:at + count, :]
                cos, sin = (trig[:, 2 * which + k, :].unsqueeze(1).to_broadcast([P, count, T])
                            for k in range(2))
                y = rotated[:, n % 2, 0:count * T].rearrange("p (b t) -> p b t", b=count)
                dve.wait_ge(sem("rot_ps"), n + 1)
                nc.vector.tensor_tensor(
                    y, ps[:, 4 + n % 2, 0:count * T].rearrange("p (b t) -> p b t", b=count), sin,
                    ALU.mult)
                settle(nc.vector.tensor_tensor(x, x, cos, ALU.mult))
                nc.vector.tensor_tensor(x, x, y, ALU.add).then_inc(sem("roped"), 1)

            def soft_max(h):
                dve.wait_ge(sem("logit_ps"), h + 1)
                if h >= 2:
                    dve.wait_ge(sem("turned_ps"), h - 1)
                mask = even_masks[:, 1 if h < HEADS else 2, :]
                settle(nc.vector.scalar_tensor_tensor(
                    out=probs[:, h % 2, :], in0=ps[:, 2 + h % 2, 0:384],
                    scalar=A_SCALE if h < HEADS else B_SCALE, in1=mask, op0=ALU.mult, op1=ALU.add))
                for m in range(2):
                    last = nc.vector.tensor_reduce(neg_max[:, h, m:m + 1],
                                                   probs[:, h % 2, 128 * m:128 + 256 * m],
                                                   AX.X, ALU.max, negate=True)
                last.then_inc(sem("max_ready"), 1)

            def soft_norm(h):
                dve.wait_ge(sem("exp_ready"), h + 1)
                tiles = [probs[:, h % 2, 128 * m:128 + 256 * m] for m in range(2)]
                if h < HEADS:
                    for m in range(2):
                        last = nc.vector.tensor_tensor_reduce(
                            out=tiles[m], in0=tiles[m],
                            in1=even_masks[:, 0, 128 * m:128 + 256 * m], scale=1.0, scalar=0.0,
                            op0=ALU.mult, op1=ALU.add, accum_out=row_sum[:, h, m:m + 1])
                    settle(last)
                settle(nc.vector.reciprocal(inv_sum[:, h, :], row_sum[:, h, :]))
                for m in range(2):
                    last = nc.vector.tensor_scalar(tiles[m], tiles[m], inv_sum[:, h, m:m + 1], None,
                                                   ALU.mult)
                last.then_inc(sem("probs_ready"), 1)

            def head_lo(layer, h):
                dve.wait_ge(sem(f"heads_hi{layer}"), h + 1)
                nc.vector.tensor_tensor(xT[:, h, 1, :], ps[:, 6 + h % 2, 0:T],
                                        xT[:, h, 0, :].bitcast(F32), ALU.subtract).then_inc(
                                            sem(f"heads_lo{layer}"), 1)

            def stick_rest(h):
                r = h % 2
                dve.wait_ge(sem("abs_ready"), h + 1)
                nc.vector.tensor_scalar(z_max[:, r, :], ps[:, 2 + r, 0:384], 0.0, None,
                                        ALU.max).then_inc(sem("zmax_ready"), 1)
                dve.wait_ge(sem("log_ready"), h + 1)
                dve.wait_ge(sem("zmax_ready"), h + 1)
                settle(nc.vector.tensor_tensor(z_max[:, r, :], z_max[:, r, :], z_log[:, r, :],
                                               ALU.add))
                if h >= 2:
                    dve.wait_ge(sem("suffix_ps"), h - 1)
                nc.vector.tensor_tensor(log_rest[:, r, :], z_max[:, r, :], neg_mask,
                                        ALU.mult).then_inc(sem("rest_ready"), 1)

            def top16(values, cut, v, i, rows):
                for s in rows:
                    last = nc.vector.max(v(s)[:, 0:8], values[:, s, :])
                settle(last)
                for s in rows:
                    nc.vector.max_index(i(s)[:, 0:8], v(s)[:, 0:8], values[:, s, :])
                    last = nc.vector.match_replace(cut[:, s, :], v(s)[:, 0:8], values[:, s, :],
                                                   REPLACED)
                settle(last)
                for s in rows:
                    last = nc.vector.max(v(s)[:, 8:16], cut[:, s, :])
                settle(last)
                for s in rows:
                    last = nc.vector.max_index(i(s)[:, 8:16], v(s)[:, 8:16], cut[:, s, :])
                return last

            def pick(layer, n):
                if n == 0:
                    dve.wait_ge(sem(f"scores{layer}"), 8)
                if n < 16:
                    settle(top16(scores, scores_cut, lambda s: top_v[:, s, :],
                                 lambda s: top_i[:, s, :], (2 * n, 2 * n + 1)))
                elif n == 16:
                    nc.vector.tensor_copy(top_f, top_i.rearrange("p s k -> p (s k)"))
                    sides = top_v.rearrange("p (m h two) k -> p m h two k", m=2, two=2)
                    for m in range(2):
                        last = nc.vector.tensor_tensor(
                            cand[:, 8 * m:8 * m + 8, :].rearrange("p h (a b) -> p h a b", a=TOPK),
                            sides[:, m, :, 0, :].unsqueeze(3).to_broadcast([P, HEADS, TOPK, TOPK]),
                            sides[:, m, :, 1, :].unsqueeze(2).to_broadcast([P, HEADS, TOPK, TOPK]),
                            ALU.add)
                    settle(last)
                elif n < 33:
                    settle(top16(cand, cand_cut, lambda s: best_v[:, s, :],
                                 lambda s: best_i[:, TOPK * s:TOPK * s + TOPK], (n - 17,)))
                elif n == 33:
                    nc.vector.tensor_tensor(
                        shifted.rearrange("p m h k -> p (m h) k"), best_v,
                        best_v[:, :, 0:1].to_broadcast([P, 2 * HEADS, TOPK]),
                        ALU.subtract).then_inc(sem(f"shifted{layer}"), 1)
                    nc.vector.tensor_scalar(rank_i[:, 0, :], best_i, 4, None,
                                            ALU.logical_shift_right)
                    settle(nc.vector.tensor_scalar(rank_i[:, 1, :], best_i, 15, None,
                                                   ALU.bitwise_and))
                    settle(nc.vector.tensor_copy(
                        rank_f.rearrange("p s m n -> p (s m n)"),
                        rank_i.rearrange("p s n -> p (s n)")))
                else:
                    turn, stage_n = divmod(n - 34, 3)
                    m, side = divmod(turn, 2)
                    eq = match.rearrange("p (n a) -> p n a", a=TOPK)
                    by_head = match.rearrange("p (h k a) -> p h k a", h=HEADS, k=TOPK)
                    keys = top_f.rearrange("p (m h two k) -> p m h two k", m=2, h=HEADS, two=2)
                    if stage_n == 0:
                        settle(nc.vector.tensor_tensor(
                            eq, iota[:, 0:TOPK].unsqueeze(1).to_broadcast([P, P, TOPK]),
                            rank_f[:, side, m, :].unsqueeze(2).to_broadcast([P, P, TOPK]),
                            ALU.is_equal))
                    elif stage_n == 1:
                        settle(nc.vector.tensor_tensor(
                            by_head, by_head, keys[:, m, :, side, :].unsqueeze(2).to_broadcast(
                                [P, HEADS, TOPK, TOPK]), ALU.mult))
                    else:
                        settle(nc.vector.tensor_reduce(picked[:, m, side, :], eq, AX.X, ALU.add))
                if n == PICK_PARTS - 1:
                    dve.wait_ge(sem(f"gate_exp{layer}"), 1)
                    settle(nc.vector.reciprocal(gate_inv, gate_sum))
                    for m in range(2):
                        g = picked[:, m, 2, :].rearrange("p (h k) -> p h k", h=HEADS)
                        last = nc.vector.tensor_tensor(
                            g, g, gate_inv[:, m, :].unsqueeze(2).to_broadcast([P, HEADS, TOPK]),
                            ALU.mult)
                    last.then_inc(sem(f"picks_done{layer}"), 1)

            def experts(layer):
                name = f"u{layer}"

                def splits(b):
                    split_lo(b.times(2).plus(base[name]))
                    split_lo(b.times(2).plus(base[name] + 1))

                def hots(late, g):
                    k = group_at(layer, late, g)
                    wait_round(dve, group_ps[k.slot(2)], k.turn(2))
                    for j in range(GROUP):
                        tok = g.times(GROUP).plus(j).index()
                        nc.vector.tensor_scalar(
                            hot1[:, k.slot(2), j, :], iota, picks[:, 0, bass.ds(tok, 1)],
                            picks[:, 2, bass.ds(tok, 1)], ALU.is_equal, ALU.mult)
                    first, width = (0, CUT) if late else (CUT, P - CUT)
                    nc.vector.tensor_tensor(
                        hot2[:, k.slot(2), 0:GROUP * width].rearrange("p (t i) -> p t i", t=GROUP),
                        iota[:, first:first + width].unsqueeze(1).to_broadcast([P, GROUP, width]),
                        picks[:, 1, bass.ds(g.times(GROUP).index(), GROUP)].unsqueeze(2)
                        .to_broadcast([P, GROUP, width]), ALU.is_equal).then_inc(
                            hots_ready[k.slot(2)], 1)

                def building(n):
                    for r in range(2):
                        b = n.times(2).plus(PICK_END + r)
                        splits(b)
                        add_up(name, b.plus(-1), 0)
                        for j in range(2):
                            hots(0, n.times(4).plus(2 * r + j))

                def late_add(b):
                    k = b.plus(first_block[name])
                    dve.wait_ge(half_ready[k.slot(2)], k.turn(2, 1))
                    nc.vector.tensor_tensor(half_sum[:, k.slot(2), :], ps[:, k.slot(2), 0:T],
                                            half_sum[:, k.slot(2), :], ALU.add).then_inc(
                                                bank_free[k.slot(2)], 1)

                def late_gate(b):
                    k = b.plus(first_block[name])
                    dve.wait_ge(sem(f"late_gelu{layer}"), b.plus(-CUT).turn(1, 1))
                    nc.vector.tensor_tensor(arena[:, b.index(), :], arena[:, b.index(), :],
                                            half_sum[:, k.slot(2), :], ALU.mult).then_inc(
                                                half_free[b.slot(2)], 1)

                def gate(g):
                    k = group_at(layer, 1, g)
                    dve.wait_ge(group_ps[k.slot(2)], k.turn(2, 1))
                    h = by_group[:, 0:CUT, g.index(), :]
                    c = ps[:, 2 + k.slot(2), 0:GROUP * CUT].rearrange("p (t i) -> p i t", t=GROUP)
                    nc.vector.tensor_tensor(h, c, h, ALU.mult).then_inc(group_out[k.slot(2)], 1)

                def late(n):
                    for r in range(LATE_CHUNK):
                        b = n.times(LATE_CHUNK).plus(CUT + r)
                        start = n.i is None and n.c == 0
                        splits(b)
                        if start and r == 0:
                            add_up(name, b.plus(-1), 0)
                        else:
                            late_add(b.plus(-1))
                            if start and r == 2:
                                for s in range(2):
                                    dve.wait_ge(group_out[s], GROUPS // 2 * (2 * layer + 1))
                                dve.wait_ge(sem(f"gelu{layer}"), CUT)
                            if not (start and r == 1):
                                late_gate(b.plus(-2))
                        here = n.times(LATE_GROUPS).plus(2 * r - 4)
                        if r == 0 and not start or r > 2:
                            for j in range(2):
                                gate(here.plus(j - 2) if r else here.plus(j + 2))
                        if r >= 2:
                            for j in range(2):
                                hots(1, here.plus(j))

                splits(At(0))
                for b in range(1, PICK_END):
                    splits(At(b))
                    add_up(name, At(b - 1), 0)
                    if b <= PICK_PARTS:
                        pick(layer, b - 1)
                dve.wait_ge(sem(f"picks_T{layer}"), 1)
                repeat(dve, 0, GROUPS // 4, 1, building, peel=1)
                repeat(dve, 0, LATE_CHUNKS, 1, late, peel=1)
                for g in (GROUPS - 2, GROUPS - 1):
                    gate(At(g))
                late_add(At(P - 1))
                late_gate(At(P - 2))
                late_gate(At(P - 1))

            def values(layer):
                name = f"v{layer}"

                def h_lo(b):
                    dve.wait_ge(sem(f"h_hi{layer}"), b.turn(1, 1))
                    nc.vector.tensor_tensor(xT[:, b.slot(2), 1, :], arena[:, b.index(), :],
                                            xT[:, b.slot(2), 0, :].bitcast(F32),
                                            ALU.subtract).then_inc(sem(f"h_lo{layer}"), 1)

                def row(b, more=True):
                    split_lo(b.times(2).plus(base[name]))
                    split_lo(b.times(2).plus(base[name] + 1))
                    if more:
                        h_lo(b.plus(1))

                h_lo(At(0))
                repeat(dve, 0, P - 2, 2, row)
                row(At(P - 2))
                row(At(P - 1), False)

            nc.vector.memset(ln_eps, LN_EPS)
            nc.vector.memset(rms_eps, RMS_EPS).then_inc(sem("eps_set"), 1)
            x_lo(0)
            feature("even_in", RAW)
            token_splits("even_v")
            latent()
            all_added("even_in")
            for n in range(8):
                rotate(n, Q_AT + 2 * n, 2, 0)
            rotate(8, KR_AT, 1, 1)
            for n in range(2):
                rotate(9 + n, QB + 8 + 2 * n, 2, 1)
            soft_max(0)
            for h in range(2 * HEADS):
                if h + 1 < 2 * HEADS:
                    soft_max(h + 1)
                soft_norm(h)
                if h:
                    head_lo(0, h - 1)
            head_lo(0, 2 * HEADS - 1)
            token_splits("even_out")
            layer_norm(0)
            x_lo(1)
            for layer in range(2):
                feature(f"query{layer}", QT_AT)
                dve.wait_ge(sem(f"kept{2 * layer}"), 16)
                experts(layer)
                values(layer)
                layer_norm(2 * layer + 1)
                if layer == 0:
                    x_lo(2)
                    dve.wait_ge(sem("kept1"), 16)
                    feature("odd_in", OQ_AT)
                    all_added("odd_in")
                    q = blocks(OQ_AT, 16)
                    nc.vector.tensor_scalar(q, q, A_SCALE, None, ALU.mult).then_inc(
                        sem("q_scaled"), 1)
                    token_splits("odd_v")
                    dve.wait_ge(sem("odd_in"), 16)
                    for h in range(C_HEADS):
                        stick_rest(h)
                        if h:
                            head_lo(1, h - 1)
                    head_lo(1, C_HEADS - 1)
                    token_splits("odd_out")
                    layer_norm(2)
                    x_lo(3)

        @block.tensor
        def _(pe):
            def mm(out, lhs, rhs, start, stop):
                return nc.tensor.matmul(out, lhs, rhs, start=start, stop=stop)

            def turn_x(k, source):
                for g in range(8):
                    m, q = divmod(g, 4)
                    if g >= 2:
                        pe.wait_ge(sem(f"xt_lo{k}"), g - 1)
                    for c in range(4):
                        last = nc.tensor.transpose(
                            ps[:, 2 + g % 2, P * c:P * c + P],
                            source[:, m, (4 * q + c) * P:(4 * q + c + 1) * P], ident)
                    last.then_inc(sem(f"xt_ps{k}"), 1)
                pe.wait_ge(sem(f"xt_lo{k}"), 8)

            def feature_block(name, b):
                k = b.plus(first_block[name])
                bank = ps[:, k.slot(2), :]
                wait_round(pe, bank_free[k.slot(2)], k.turn(2))
                for q in range(4):
                    h = b.times(4).plus(2 * base[name] + q)
                    pe.wait_ge(lo_ready[h.slot(SPLITS)], h.turn(SPLITS, 1))
                    hi = w_hi[:, h.slot(SPLITS), :].rearrange("p (k n) -> p k n", k=4)
                    lo = w_lo[:, h.slot(SPLITS), :].rearrange("p (k n) -> p k n", k=4)
                    for c in range(4):
                        kc = 4 * q + c
                        both = xT[:, kc, :, :].rearrange("p s t -> p (s t)")
                        if kc < KC - 1:
                            mm(bank, hi[:, c, :], both, kc == 0, False)
                            last = mm(bank[:, 0:T], lo[:, c, :], xT[:, kc, 0, :], False, False)
                        else:
                            mm(bank[:, 0:T], lo[:, c, :], xT[:, kc, 0, :], False, False)
                            last = mm(bank, hi[:, c, :], both, False, True)
                    last.then_inc(used[h.slot(SPLITS)], 1)

            def feature(name):
                repeat(pe, 0, n_blocks(name), 2, lambda b: feature_block(name, b),
                       peel=0 if first_block[name] else 2)

            def token_unit(g, lhs, banks, start, stop):
                for c in range(2):
                    h = g.times(2).plus(c)
                    pe.wait_ge(lo_ready[h.slot(SPLITS)], h.turn(SPLITS, 1))
                    hi, lo = w_hi[:, h.slot(SPLITS), :], w_lo[:, h.slot(SPLITS), :]
                    for m in range(2):
                        xh, xl = (lhs[:, s, m * P:(m + 1) * P] for s in range(2))
                        out = ps[:, banks[m] + c, :]
                        mm(out, xh, hi, start, False)
                        mm(out, xh, lo, False, False)
                        last = mm(out, xl, hi, False, stop)
                    last.then_inc(used[h.slot(SPLITS)], 1)

            def token(name, halves, first_bank):
                for kc in range(KC):
                    for half in range(halves):
                        g = At(base[name] + halves * kc + half)
                        banks = [first_bank + 2 * halves * m + 2 * half for m in range(2)]
                        token_unit(g, xT[:, kc, :, :], banks, kc == 0, kc == KC - 1)

            def token_done(name, done, n=1):
                h = At(2 * (base[name] + t[name].shape[0]) - 1)
                pe.wait_ge(used[h.slot(SPLITS)], h.turn(SPLITS, 1))
                pe.sem_inc(sem(done), n)

            def latent():
                pe.wait_ge(sem("sq"), 1)
                for k in range(4):
                    mm(ps[:, 2, 0:T], ones, squares[:, T * k:T * k + T], k == 0, k == 3)
                for k in range(2):
                    last = mm(ps[:, 2, T:2 * T], ones, squares[:, T * (4 + k):T * (5 + k)], k == 0,
                              k == 1)
                last.then_inc(sem("sq_ps"), 1)
                pe.wait_ge(sem("latents"), 1)
                for n in range(14):
                    if n >= 2:
                        pe.wait_ge(sem("mla_out"), n - 1)
                    bank = ps[:, 2 + n % 2, :]
                    if n < 10:
                        w, kc, at = (w_qb, 4, CQN) if n < 6 else (w_kvb, 2, CKVN)
                        for j in range(2):
                            col = P * (2 * (n if n < 6 else n - 6) + j)
                            for k in range(kc):
                                last = mm(bank[:, T * j:T * j + T], w[:, k, col:col + P],
                                          arena[:, at + k, :], k == 0, k == kc - 1)
                    else:
                        m, c = divmod(n - 10, 2)
                        for k in range(2):
                            last = mm(bank, arena[:, CKVN + k, m * P:(m + 1) * P],
                                      w_kvb[:, k, 1024 + 512 * c:1536 + 512 * c], k == 0, k == 1)
                    last.then_inc(sem("mla_ps"), 1)

            def rotate(n, at, count, rot):
                if n >= 2:
                    pe.wait_ge(sem("roped"), n - 1)
                mm(ps[:, 4 + n % 2, 0:count * T], rot, blocks(at, count), True, True).then_inc(
                    sem("rot_ps"), 1)

            def logits(h):
                bank = ps[:, 2 + h % 2, :]
                if h >= 2:
                    pe.wait_ge(sem("max_ready"), h - 1)
                if h < HEADS:
                    parts = [(arena[:, Q_AT + h, :], arena[:, K_AT + h, :])]
                else:
                    j = h - HEADS
                    half = slice(ROPE * (j % 2), ROPE * (j % 2) + ROPE)
                    parts = [(arena[:, QB + j, :], arena[:, KN + j, :]),
                             (arena[half, QB + 8 + j // 2, :], arena[half, KR_AT, :])]
                for m in range(2):
                    out = bank[:, 128 * m:128 + 256 * m]
                    for n, (q, k) in enumerate(parts):
                        last = mm(out, q[:, m * P:(m + 1) * P], k[:, 0:P * (m + 1)], n == 0,
                                  n == len(parts) - 1)
                last.then_inc(sem("logit_ps"), 1)

            def turn_probs(h):
                pe.wait_ge(sem("probs_ready"), h + 1)
                if h >= 2:
                    pe.wait_ge(sem("turned"), h - 1)
                for b in range(3):
                    last = nc.tensor.transpose(ps[:, 4 + h % 2, P * b:P * b + P],
                                               probs[:, h % 2, P * b:P * b + P], ident)
                last.then_inc(sem("turned_ps"), 1)

            def head(layer, h, weights, ready, val, col):
                pe.wait_ge(sem(ready), h + 1)
                if h >= 2:
                    pe.wait_ge(sem(f"heads_lo{layer}"), h - 1)
                bank = ps[:, 6 + h % 2, :]
                mm(bank[:, 0:T], val[:, 0, col:col + P], weights[:, h % 2, 0:T], True, False)
                mm(bank[:, P:T], val[:, 1, col:col + P], weights[:, h % 2, T:384], False,
                   True).then_inc(sem(f"head_ps{layer}"), 1)

            def head_even(h):
                head(0, h, probs_t, "turned", val_a if h < HEADS else val_b, P * (h % HEADS))

            def stick_z(h):
                if h >= 2:
                    pe.wait_ge(sem("zmax_ready"), h - 1)
                bank = ps[:, 2 + h % 2, :]
                q, k = arena[:, OQ_AT + h, :], arena[:, OK_AT + h, :]
                mm(bank[:, 0:T], k[:, 0:P], q, True, True)
                mm(bank[:, T:384], k[:, P:T], q[:, P:T], True, True).then_inc(sem("z_ps"), 1)

            def stick_suffix(h):
                pe.wait_ge(sem("rest_ready"), h + 1)
                if h >= 2:
                    pe.wait_ge(sem("att_ready"), h - 1)
                bank, rest = ps[:, 4 + h % 2, :], log_rest[:, h % 2, :]
                q, k = arena[:, OQ_AT + h, :], arena[:, OK_AT + h, :]
                mm(bank[:, 0:T], tri, rest[:, 0:T], True, False)
                mm(bank[:, P:T], ones, rest[:, T:384], False, False)
                mm(bank[:, 0:P], ident, diag_mask, False, False)
                mm(bank[:, 0:T], k[:, 0:P], q, False, True)
                mm(bank[:, T:384], tri, rest[:, T:384], True, False)
                mm(bank[:, T:384], ident, diag_mask, False, False)
                mm(bank[:, T:384], k[:, P:T], q[:, P:T], False, True).then_inc(sem("suffix_ps"), 1)

            def score(layer):
                pe.wait_ge(sem(f"keys_in{layer}"), 16)
                for n in range(8):
                    if n >= 2:
                        pe.wait_ge(sem(f"scores{layer}"), n - 1)
                    m, g = divmod(n, 4)
                    for j in range(4):
                        s = 4 * g + j
                        last = mm(ps[:, 2 + n % 2, P * j:P * j + P],
                                  arena[:, QT_AT + s, m * P:(m + 1) * P], keys_t[:, s, :],
                                  True, True)
                    last.then_inc(sem(f"score_ps{layer}"), 1)

            def experts(layer):
                name = f"u{layer}"

                def one(b):
                    feature_block(name, b)

                def turn_picks():
                    pe.wait_ge(sem(f"picks_done{layer}"), 1)
                    for m in range(2):
                        for w in range(3):
                            last = nc.tensor.transpose(ps[:, 2 + m, P * w:P * w + P],
                                                       picked[:, m, w, :], ident)
                    last.then_inc(sem(f"picks_ps{layer}"), 1)

                def group(late, g):
                    k = group_at(layer, late, g)
                    wait_round(pe, group_out[k.slot(2)], k.turn(2))
                    pe.wait_ge(hots_ready[k.slot(2)], k.turn(2, 1))
                    width = CUT if late else P - CUT
                    for j in range(GROUP):
                        last = mm(ps[:, 2 + k.slot(2), width * j:width * j + width],
                                  hot1[:, k.slot(2), j, :],
                                  hot2[:, k.slot(2), width * j:width * j + width], True, True)
                    last.then_inc(group_ps[k.slot(2)], 1)

                def building(n):
                    for r in range(2):
                        one(n.times(2).plus(PICK_END + r))
                        for j in range(2):
                            group(0, n.times(4).plus(2 * r + j))

                def late(n):
                    for r in range(LATE_CHUNK):
                        one(n.times(LATE_CHUNK).plus(CUT + r))
                        if r >= 2:
                            for j in range(2):
                                group(1, n.times(LATE_GROUPS).plus(2 * r - 4 + j))

                repeat(pe, 0, PICK_PARTS, 2, one)
                one(At(PICK_PARTS))
                turn_picks()
                one(At(PICK_PARTS + 1))
                repeat(pe, 0, GROUPS // 4, 1, building, peel=1)
                repeat(pe, 0, LATE_CHUNKS, 1, late)

            def values(layer):
                name = f"v{layer}"

                def row(b, start=False, stop=False):
                    pe.wait_ge(sem(f"h_lo{layer}"), b.turn(1, 1))
                    for half in range(2):
                        token_unit(b.times(2).plus(base[name] + half), xT[:, b.slot(2), :, :],
                                   [2 * half, 4 + 2 * half], start, stop)

                for s in range(2):
                    pe.wait_ge(group_out[s], GROUPS * (layer + 1))
                    end = first_block[f"u{layer}"] + P
                    pe.wait_ge(bank_free[s], (end - s + 1) // 2)
                row(At(0), start=True)
                row(At(1))
                repeat(pe, 2, P - 2, 2, row)
                row(At(P - 2))
                row(At(P - 1), stop=True)

            pe.wait_ge(sem("const_in"), 16)
            pe.wait_ge(sem("x_in"), 16)
            turn_x(0, x_first)
            feature("even_in")
            token("even_v", 1, 4)
            token_done("even_v", "va_ps")
            latent()
            pe.wait_ge(sem("mla_out"), 14)
            for n in range(8):
                rotate(n, Q_AT + 2 * n, 2, rot_a)
            rotate(8, KR_AT, 1, rot_b)
            for n in range(2):
                rotate(9 + n, QB + 8 + 2 * n, 2, rot_b)
            pe.wait_ge(sem("roped"), 11)
            pe.wait_ge(sem("va_out"), 1)
            logits(0)
            for h in range(2 * HEADS):
                if h + 1 < 2 * HEADS:
                    logits(h + 1)
                turn_probs(h)
                if h:
                    head_even(h - 1)
            head_even(2 * HEADS - 1)
            pe.wait_ge(sem("heads_lo0"), 16)
            token("even_out", 2, 0)
            token_done("even_out", "y_ps0", 8)
            pe.wait_ge(sem("ln_done0"), 1)
            turn_x(1, residual)
            for layer in range(2):
                feature(f"query{layer}")
                pe.wait_ge(bank_free[0], (first_block[f"query{layer}"] + 16 + 1) // 2)
                pe.wait_ge(bank_free[1], (first_block[f"query{layer}"] + 16) // 2)
                pe.sem_inc(sem(f"qT_ready{layer}"), 1)
                score(layer)
                experts(layer)
                values(layer)
                token_done(f"v{layer}", f"y_ps{2 * layer + 1}", 8)
                if layer == 0:
                    pe.sem_inc(sem("pe_v_done0"), 1)
                    pe.wait_ge(sem("ln_done1"), 1)
                    turn_x(2, residual)
                    feature("odd_in")
                    pe.wait_ge(bank_free[0], (first_block["odd_in"] + 32 + 1) // 2)
                    pe.wait_ge(bank_free[1], (first_block["odd_in"] + 32) // 2)
                    token("odd_v", 2, 0)
                    token_done("odd_v", "vc_ps")
                    pe.wait_ge(sem("vc_out"), 1)
                    pe.wait_ge(sem("q_scaled"), 1)
                    pe.wait_ge(sem("odd_in"), 16)
                    stick_z(0)
                    for h in range(C_HEADS):
                        if h + 1 < C_HEADS:
                            stick_z(h + 1)
                        stick_suffix(h)
                        if h:
                            head(1, h - 1, att, "att_ready", val_c, P * (h - 1))
                    head(1, C_HEADS - 1, att, "att_ready", val_c, P * (C_HEADS - 1))
                    pe.wait_ge(sem("heads_lo1"), 16)
                    token("odd_out", 2, 0)
                    token_done("odd_out", "y_ps2", 8)
                    pe.wait_ge(sem("ln_done2"), 1)
                    turn_x(3, residual)


def feature_units(w):
    n = w.shape[1] // P
    return np.ascontiguousarray(
        w.reshape(2, 8, P, n, P).transpose(3, 0, 2, 1, 4).reshape(2 * n, P, UNIT))


def token_units(w):
    n = w.shape[1] // UNIT
    return np.ascontiguousarray(w.reshape(KC, P, n, UNIT).transpose(0, 2, 1, 3).reshape(KC * n, P, UNIT))


def shape_constants():
    eye = np.eye(P, dtype=np.float32)
    iota = np.tile(np.arange(P, dtype=np.float32), (P, 1))
    ones = np.ones((P, P), np.float32)

    def rotation(half):
        r = np.zeros((P, P), np.float32)
        for m in range(P):
            low = m % (2 * half) < half
            r[m + half if low else m - half, m] = -1.0 if low else 1.0
        return r

    const = np.stack([eye, ones, iota], 1)
    rotations = np.stack([rotation(64), rotation(32)], 1)

    def angles(half):
        inv = np.float32(10000.0) ** (-np.arange(half, dtype=np.float32) / np.float32(half))
        ang = (np.arange(T, dtype=np.float32)[:, None] * inv[None, :]).astype(np.float32).T
        ang = np.tile(ang, (P // half, 1))
        return np.cos(ang).astype(np.float32), np.sin(ang).astype(np.float32)

    trig = np.stack([*angles(64), *angles(32)], 1)
    q, k = np.arange(T)[:, None], np.arange(T)[None, :]
    back = q - k
    count = (((back >= 0) & (back <= 128)).astype(np.float32) + ((back >= 0) & (back % 4 == 0))
             + ((back >= 0) & (back % 16 == 0)))

    def tiles(a):
        return np.concatenate([a[0:P, 0:P], a[P:T, 0:T]], 1)

    even_masks = np.stack([tiles(count), tiles(np.where(count > 0, 0.0, NEG)),
                           tiles(np.where(back >= 0, 0.0, NEG))], 1).astype(np.float32)
    j, s = np.arange(P)[:, None], np.arange(P)[None, :]
    tri = (j >= s).astype(np.float32)
    earlier = (j < s)
    diag = np.where(earlier, 0.0, NEG).astype(np.float32)
    neg = -np.concatenate([earlier, np.ones((P, P)), earlier], 1).astype(np.float32)
    odd_consts = np.concatenate([tri, diag, neg], 1).astype(np.float32)
    return {"const": const, "rotations": rotations, "trig": trig, "even_masks": even_masks, "odd_consts": odd_consts}


def layout(i):
    i = {k: np.asarray(v) for k, v in i.items()}
    w = i["a_w_in"][0]
    a, cq, ckv = 1024, 3072, 3584
    kr = w[:, 3840:3904]
    feats = np.concatenate([w[:, 0:2 * a], w[:, cq:ckv], w[:, ckv:3840], kr, kr], 1)
    wq = i["b_w_q_b"][0].reshape(4, P, HEADS, 192)
    wq = np.concatenate([wq[..., 0:P].reshape(4, P, 1024), wq[..., P:].reshape(4, P, 512)], 2)
    wkv = i["b_w_kv_b"][0].reshape(2, P, HEADS, 256)
    wkv = np.concatenate([wkv[..., 0:P].reshape(2, P, 1024), wkv[..., P:].reshape(2, P, 1024)], 2)
    c = np.ascontiguousarray
    t = {
        "x": c(i["x"].reshape(T, D)),
        "even_in": feature_units(feats), "even_v": token_units(w[:, 2 * a:3 * a]),
        "even_out": token_units(i["ab_w_out"][0]),
        "odd_in": feature_units(i["c_w_in"][0][:, 0:4096]),
        "odd_v": token_units(i["c_w_in"][0][:, 4096:]),
        "odd_out": token_units(i["c_w_out"][0]),
        "w_qb": c(wq.transpose(1, 0, 2)), "w_kvb": c(wkv.transpose(1, 0, 2)),
        "q_gain": c(i["b_q_norm"][0].reshape(4, P).T), "kv_gain": c(i["b_kv_norm"][0].reshape(2, P).T),
        "keys_t": c(i["peer_sub_keys"].reshape(2, 16, N_KEYS, P).transpose(0, 3, 1, 2)),
        "ln_gain": c(i["ln_gain"].reshape(4, D)), "ln_bias": c(i["ln_bias"].reshape(4, D)),
    }
    for n in range(2):
        t[f"query{n}"] = feature_units(i["peer_w_query"][n])
        u = i["peer_u"][n].reshape(P, P, 2, 8, P)
        t[f"u{n}"] = c(u.transpose(1, 2, 4, 3, 0)).reshape(2 * P, P, UNIT)
        v = i["peer_v"][n].reshape(P, P, 2, UNIT)
        t[f"v{n}"] = c(v.transpose(1, 2, 0, 3)).reshape(2 * P, P, UNIT)
    t.update(shape_constants())
    return t


def kernel(**inputs):
    import concourse.bacc as bacc
    from concourse.bass_utils import run_bass_kernel_spmd

    nc = bacc.Bacc("TRN2", target_bir_lowering=False, num_devices=1)
    arrays = layout(inputs)
    t = {}
    for name, a in arrays.items():
        t[name] = nc.dram_tensor(f"in_{name}", a.shape, mybir.dt.from_np(a.dtype),
                                 kind="ExternalInput").ap()
    t["kept"] = nc.dram_tensor("kept", (3, T, D), F32).ap()
    t["out"] = nc.dram_tensor("out_x", (T, D), F32, kind="ExternalOutput").ap()
    decoder(nc, t)
    r = run_bass_kernel_spmd(nc, [{f"in_{name}": a for name, a in arrays.items()}], core_ids=[0])
    return r.results[0]["out_x"].reshape(1, T, D)
```

```python
from contextlib import ExitStack

import concourse.bass as bass
import concourse.mybir as mybir
import numpy as np
from concourse.alu_op_type import AluOpType as ALU

ACT = mybir.ActivationFunctionType
AX = mybir.AxisListType
F32 = mybir.dt.float32
F32R = mybir.dt.float32r
U32 = mybir.dt.uint32

P = 128
D = 2048
T = 256
TILES = T // P
KC = D // P
UNIT = 1024
STAGES = 4
HALF = UNIT // 2
SPLITS = 4
HEADS = 8
C_HEADS = 16
TOPK = 16
N_KEYS = 128
Q_LORA = 512
KV_LORA = 256
ROPE = 64
ALPHA = float(4 ** 0.25)
LN_EPS = 1e-5
RMS_EPS = 1e-6
NEG = -1e30
REPLACED = -3.0e38
A_SCALE = float(128 ** -0.5)
B_SCALE = float((128 + 64) ** -0.5)

PICK_END = 48
GROUP = 4
GROUPS = T // GROUP
BUILD = 2
CUT = PICK_END + GROUPS // BUILD
GROUP_BANKS = 4
GATE_STEP = 38
PICK_PARTS = 46



TURN_BANKS = 6
ROPE_FROM = 4
SOFT_STEPS = 2 * HEADS + 8
STICK_STEPS = C_HEADS + 8
Z_BANKS = (2, 3, 6, 7)


class At:

    def __init__(self, c, i=None, step=0):
        self.c, self.i, self.step = c, i, step

    def plus(self, n):
        return At(self.c + n, self.i, self.step)

    def times(self, n):
        return At(self.c * n, self.i, self.step * n)

    def index(self):
        return self.c if self.i is None else self.i * self.step + self.c

    def slot(self, ring):
        return self.c % ring

    def turn(self, ring, more=0, each=1):
        c = (self.c // ring + more) * each
        return c if self.i is None else self.i * (self.step // ring * each) + c


def repeat(eng, first, last, step, body, peel=0):
    for c in range(first, first + peel):
        body(At(c))
    first += peel
    n = (last - first) // step
    if n >= 2:
        with eng.Fori(0, n) as i:
            for r in range(step):
                body(At(first + r, i, step))
        first += n * step
    for c in range(first, last):
        body(At(c))


def wait_round(eng, s, turns):
    if not isinstance(turns, int) or turns > 0:
        eng.wait_ge(s, turns)


def decoder(nc, t):
    with ExitStack() as ctx:
        def sb(name, shape, dt=F32):
            return ctx.enter_context(nc.sbuf_tensor(name, shape, dt))

        sems = {}

        def sem(name):
            if name not in sems:
                sems[name] = ctx.enter_context(nc.semaphore(name))
            return sems[name]

        arena = sb("arena", [P, P, T])
        xT = sb("xT", [P, KC, 2, T], F32R)
        stage = sb("stage", [P, STAGES, UNIT])
        w_hi = sb("w_hi", [P, SPLITS, HALF], F32R)
        w_lo = sb("w_lo", [P, SPLITS, HALF], F32R)
        half_sum = sb("half_sum", [P, 2, T])
        const = sb("const", [P, 3, P])
        picks = sb("picks", [P, 3, T])
        hot1 = sb("hot1", [P, 2, GROUP, P])
        hot2 = sb("hot2", [P, 2, GROUP, P])
        small = sb("small", [P, 224])
        ps = ctx.enter_context(nc.psum_tensor("ps", [P, 8, 512], F32))

        ident, ones, iota = (const[:, k, :] for k in range(3))
        q_gain, kv_gain = small[:, 0:4], small[:, 4:6]
        neg_mean, total, var_sum, rstd = (small[:, at:at + 2] for at in (8, 10, 12, 14))
        sums = small[:, 16:24].rearrange("p (m c) -> p m c", m=2)
        neg_max = small[:, 64:96].rearrange("p (h m) -> p h m", m=2)
        row_sum = small[:, 96:128].rearrange("p (h m) -> p h m", m=2)
        inv_sum = small[:, 128:160].rearrange("p (h m) -> p h m", m=2)
        gate_sum = small[:, 160:176].rearrange("p (m h) -> p m h", m=2)
        gate_inv = small[:, 176:192].rearrange("p (m h) -> p m h", m=2)
        ln_eps, rms_eps = small[:, 192:193], small[:, 193:194]

        def blocks(first, count):
            return arena[:, first:first + count, :].rearrange("p b t -> p (b t)")

        residual = blocks(0, 16).rearrange("p (m d) -> p m d", m=2)
        gain, bias = blocks(16, 8), blocks(24, 8)
        scaled = blocks(32, 16).rearrange("p (m d) -> p m d", m=2)
        centred, deviation = blocks(80, 8), blocks(88, 8)
        RAW, Q_AT, K_AT, CQ_AT, CKV_AT, KR_AT = 0, 0, 8, 16, 20, 22
        val_a = blocks(23, 8).rearrange("p (m d) -> p m d", m=2)
        x_first = blocks(31, 16).rearrange("p (m d) -> p m d", m=2)
        CQN, CKVN, QB, KN = 31, 35, 37, 49
        val_b = blocks(57, 8).rearrange("p (m d) -> p m d", m=2)
        w_qb = blocks(65, 24).rearrange("p (k n) -> p k n", k=4)
        w_kvb = blocks(89, 16).rearrange("p (k n) -> p k n", k=2)
        even_masks = blocks(105, 5)[:, 0:1152].rearrange("p (k n) -> p k n", k=3)
        trig = arena[:, 110:114, :]
        rot_a, rot_b = hot1[:, 0, 0, :], hot1[:, 0, 1, :]
        probs = blocks(114, 6).rearrange("p (r n) -> p r n", r=4)
        probs_t = blocks(120, 3).rearrange("p (r n) -> p r n", r=2)
        squares = blocks(114, 6)
        rms = arena[:, 126:128, :]
        rotated, rotated_b = (blocks(at, 4).rearrange("p (r n) -> p r n", r=2)
                              for at in (120, CQN))
        OQ_AT, OK_AT = 0, 16
        val_c = blocks(32, 16).rearrange("p (m d) -> p m d", m=2)
        odd_consts = blocks(48, 2)
        neg_tri, diag_mask, neg_ones = (odd_consts[:, P * k:P * k + P] for k in range(3))

        def ring2(first):
            return blocks(first, 3).rearrange("p (r n) -> p r n", r=2)

        z_abs, z_exp, z_log, rest, att = (ring2(51 + 3 * k) for k in range(5))
        z_kept = blocks(66, 9).rearrange("p (r n) -> p r n", r=6)
        QT_AT = 48
        keys_t = blocks(64, 8).rearrange("p (s n) -> p s n", s=16)
        scores = blocks(72, 16).rearrange("p (s n) -> p s n", s=32)
        scores_cut = blocks(88, 16).rearrange("p (s n) -> p s n", s=32)
        top_v = blocks(104, 2).rearrange("p (s k) -> p s k", s=32)
        top_i = blocks(106, 2).bitcast(U32).rearrange("p (s k) -> p s k", s=32)
        top_f = blocks(108, 2)
        cand = blocks(110, 16).rearrange("p (s n) -> p s n", s=16)
        cand_cut = blocks(48, 16).rearrange("p (s n) -> p s n", s=16)
        best_v = blocks(126, 1).rearrange("p (s k) -> p s k", s=16)
        best_i = blocks(127, 1).bitcast(U32)
        rank_i = blocks(64, 2).bitcast(U32).rearrange("p (s n) -> p s n", s=2)
        rank_f = blocks(66, 2).rearrange("p (s m n) -> p s m n", s=2, m=2)
        picked = blocks(68, 3).rearrange("p (m w n) -> p m w n", m=2, w=3)
        shifted = blocks(71, 1).rearrange("p (m h k) -> p m h k", m=2, h=HEADS)
        match = blocks(72, 8)
        by_group = arena[:, :, :].rearrange("p i (g t) -> p i g t", t=GROUP)

        order = [("even_in", "even_in"), ("even_v", "even_v"), ("even_out", "even_out"),
                 ("query0", "query0"), ("u0", "u0"), ("v0", "v0"),
                 ("odd_in", "odd_in"), ("odd_v", "odd_v"), ("odd_out", "odd_out"),
                 ("query1", "query1"), ("u1", "u1"), ("v1", "v1")]
        base, at = {}, 0
        for name, _ in order:
            base[name] = at
            at += t[name].shape[0]
        FEATURE = ["even_in", "query0", "u0", "odd_in", "query1", "u1"]
        first_block, at = {}, 0
        for name in FEATURE:
            first_block[name] = at
            at += t[name].shape[0] // 2

        def n_blocks(name):
            return t[name].shape[0] // 2

        staged = [sem(f"staged{s}") for s in range(STAGES)]
        hi_ready = [sem(f"hi_ready{s}") for s in range(SPLITS)]
        lo_ready = [sem(f"lo_ready{s}") for s in range(SPLITS)]
        used = [sem(f"used{s}") for s in range(SPLITS)]
        half_ready = [sem(f"half_ready{s}") for s in range(2)]
        bank_free = [sem(f"bank_free{s}") for s in range(2)]
        half_free = [sem(f"half_free{s}") for s in range(2)]
        hots_equal = [sem(f"hots_equal{s}") for s in range(2)]
        hots_ready = [sem(f"hots_ready{s}") for s in range(2)]
        group_ps = [sem(f"group_ps{s}") for s in range(2)]
        group_kept = [sem(f"group_kept{s}") for s in range(2)]
        group_out = [sem(f"group_out{s}") for s in range(2)]

        def group_at(layer, g):
            return g.plus(GROUPS * layer)

        def built_before(b):
            return min(max(GROUP * BUILD * (b - PICK_END + 1), 0), T)

        def column_bank(m, c):
            return 4 * m + (c + 2) % 4

        def rotate_bank(n):
            return 0 if n == HEADS else 6 + n % 2

        def beside(k, lags, n):
            return [(part, k - lag) for part, lag in lags if 0 <= k - lag < n]

        block = ctx.enter_context(nc.Block())

        @block.sync
        def _(sp):
            sp.dma_start(const[:, :, :], t["const"]).then_inc(sem("const_in"), 16)
            for n in range(4):
                m, c = divmod(n, 2)
                half = slice(UNIT * c, UNIT * c + UNIT)
                sp.dma_start(x_first[:, m, half], t["x"][m * P:(m + 1) * P, half]).then_inc(
                    sem(f"x_in{n}"), 16)
                if n == 1:
                    sp.dma_start(stage[:, 0, :], t[order[0][0]][0]).then_inc(staged[0], 16)
            for name, _ in order:
                units = t[name]

                def load(a, units=units, name=name):
                    g = a.plus(base[name])
                    second = g.times(2).plus(1)
                    wait_round(sp, lo_ready[second.slot(SPLITS)],
                               second.turn(SPLITS, 1 - 2 * STAGES // SPLITS))
                    sp.dma_start(stage[:, g.slot(STAGES), :], units[a.index()]).then_inc(
                        staged[g.slot(STAGES)], 16)

                if base[name]:
                    repeat(sp, 0, units.shape[0], STAGES, load)
                else:
                    repeat(sp, 1, units.shape[0], STAGES, load, peel=STAGES - 1)
            for n in range(4):
                m, c = divmod(n, 2)
                half = slice(UNIT * c, UNIT * c + UNIT)
                sp.wait_ge(sem("ln_out3"), 2 * n + 2)
                sp.dma_start(t["out"][m * P:(m + 1) * P, half], residual[:, m, half]).then_inc(
                    sem("out_done"), 16)
            sp.wait_ge(sem("out_done"), 4 * 16)

        @block.gpsimd
        def _(pool):
            def get(dst, src, s):
                pool.dma_start(dst, src).then_inc(sem(s), 16)

            pool.wait_ge(bank_free[0], 1)
            get(hot1[:, 0, 0:2, :], t["rotations"], "rot_in")
            get(trig, t["trig"], "rot_in")
            for k in range(4):
                pool.wait_ge(bank_free[0], 2 + k)
                get(w_qb[:, k, :], t["w_qb"][:, k, :], "mla_in")
            for k in range(2):
                pool.wait_ge(bank_free[0], 6 + k)
                get(w_kvb[:, k, :], t["w_kvb"][:, k, :], "mla_in")
            pool.wait_ge(bank_free[0], 8)
            get(q_gain, t["q_gain"], "mla_in")
            get(kv_gain, t["kv_gain"], "mla_in")
            get(even_masks, t["even_masks"], "mla_in")

            def norm_in(k, source, layer=None):
                rows = t["ln_gain"][k], t["ln_bias"][k]
                parts = [(residual[:, m, :], source[m * P:(m + 1) * P, :]) for m in range(2)]
                parts += [(dst, row.partition_broadcast(P)) for dst, row in zip((gain, bias), rows)]
                for n, (dst, src) in enumerate(parts):
                    if layer is not None:
                        pool.wait_ge(sem(f"h_lo{layer}"), 33 + 3 * n)
                    get(dst, src, f"ln_in{k}")

            def scale(k):
                for c in range(4):
                    part = slice(512 * c, 512 * c + 512)
                    pool.wait_ge(sem(f"ln_centred{k}"), c + 1)
                    nc.gpsimd.tensor_tensor(scaled[:, 0, part], centred[:, part], gain[:, part],
                                            ALU.mult).then_inc(sem(f"ln_scaled{k}"), 1)

            def keep(k):
                pool.wait_ge(sem(f"ln_out{k}"), 8)
                get(t["kept"][k].rearrange("(m p) d -> p m d", p=P), residual, f"kept{k}")
                pool.wait_ge(sem(f"kept{k}"), 16)

            def gates(layer):
                def group(g):
                    k = group_at(layer, g)
                    pool.wait_ge(hots_equal[k.slot(2)], k.turn(2, 1))
                    gate = picks[:, 2, bass.ds(g.times(GROUP).index(), GROUP)].unsqueeze(2)
                    nc.gpsimd.tensor_tensor(
                        hot2[:, k.slot(2), :, :], hot2[:, k.slot(2), :, :],
                        gate.to_broadcast([P, GROUP, P]), ALU.mult).then_inc(
                            hots_ready[k.slot(2)], 1)

                repeat(pool, 0, GROUPS, 2, group)

            pool.wait_ge(sem("heads_lo0"), 16)
            norm_in(0, t["x"])
            get(keys_t, t["keys_t"][0], "keys_in0")
            for layer in range(2):
                scale(2 * layer)
                keep(2 * layer)
                gates(layer)
                norm_in(2 * layer + 1, t["kept"][2 * layer], layer)
                scale(2 * layer + 1)
                if layer == 0:
                    keep(1)
                    get(odd_consts[:, 0:3 * P], t["odd_consts"], "odd_in")
                    pool.wait_ge(sem("heads_lo1"), 16)
                    norm_in(2, t["kept"][1])
                    get(keys_t, t["keys_t"][1], "keys_in1")

        @block.scalar
        def _(act):
            def half_hi(g, q):
                if q == 0:
                    act.wait_ge(staged[g.slot(STAGES)], g.turn(STAGES, 1, 16))
                h = g.times(2).plus(q)
                wait_round(act, used[h.slot(SPLITS)], h.turn(SPLITS))
                nc.scalar.activation(w_hi[:, h.slot(SPLITS), :],
                                     stage[:, g.slot(STAGES), HALF * q:HALF * q + HALF],
                                     ACT.Copy).then_inc(hi_ready[h.slot(SPLITS)], 1)

            def split_hi(g):
                for q in range(2):
                    half_hi(g, q)

            def token_splits(name, first=0, last=None):
                last = t[name].shape[0] if last is None else last
                repeat(act, base[name] + first, base[name] + last, STAGES, split_hi)

            def copy_half(name, b):
                last = b.times(4).plus(2 * base[name] + 3)
                act.wait_ge(used[last.slot(SPLITS)], last.turn(SPLITS, 1))
                k = b.plus(first_block[name])
                nc.scalar.activation(half_sum[:, k.slot(2), :], ps[:, k.slot(2), T:2 * T],
                                     ACT.Copy).then_inc(half_ready[k.slot(2)], 1)

            def feature(name, following):
                def step(b):
                    split_hi(b.times(2).plus(base[name]))
                    split_hi(b.times(2).plus(base[name] + 1))
                    copy_half(name, b.plus(-1))

                repeat(act, 1, n_blocks(name), 2, step)
                split_hi(At(base[following]))
                copy_half(name, At(n_blocks(name) - 1))

            def h_hi(layer, b):
                nc.scalar.activation(xT[:, b.slot(2), 0, :], arena[:, b.index(), :],
                                     ACT.Copy).then_inc(sem(f"h_hi{layer}"), 1)

            def experts(layer):
                name = f"u{layer}"

                def splits(b):
                    split_hi(b.times(2).plus(base[name]))
                    split_hi(b.times(2).plus(base[name] + 1))

                def wait_added(b):
                    k = b.plus(first_block[name])
                    act.wait_ge(bank_free[k.slot(2)], k.turn(2, 1))

                def gelu(b):
                    nc.scalar.activation(arena[:, b.index(), :], arena[:, b.index(), :],
                                         ACT.Gelu).then_inc(sem(f"gelu{layer}"), 1)

                def early(b):
                    splits(b)
                    wait_added(b.plus(-2))
                    copy_half(name, b.plus(-1))
                    gelu(b.plus(-2))

                def keep_c(b, j):
                    g = BUILD * (b - PICK_END) + j
                    k = group_at(layer, At(g))
                    act.wait_ge(group_ps[k.slot(2)], k.turn(2, 1))
                    c = ps[:, 2 + k.slot(GROUP_BANKS), :].rearrange("p (t i) -> p i t", t=GROUP)
                    nc.scalar.activation(by_group[:, b:P, g, :], c[:, b:P, :], ACT.Copy).then_inc(
                        group_kept[k.slot(2)], 1)

                def late_gelu(b):
                    k = b.plus(first_block[name])
                    wait_added(b)
                    first = T if b.i is not None else built_before(b.c)
                    if first < T:
                        nc.scalar.activation(arena[:, b.c, first:T], half_sum[:, k.slot(2), first:T],
                                             ACT.Gelu)
                    nc.scalar.activation(half_sum[:, k.slot(2), 0:first],
                                         half_sum[:, k.slot(2), 0:first],
                                         ACT.Gelu).then_inc(sem(f"gelu{layer}"), 1)

                def late_half(b):
                    if not (b.i is None and b.c < PICK_END + 2):
                        before = b.plus(-PICK_END + layer * (P - PICK_END))
                        act.wait_ge(half_free[before.slot(2)], before.turn(2))
                    copy_half(name, b)

                def building(b):
                    for q in range(4):
                        half_hi(At(2 * b + base[name] + q // 2), q % 2)
                        if q == 0 and b - 2 >= PICK_END:
                            keep_c(b - 2, 1)
                        if q == 2 and PICK_END <= b - 1 < CUT:
                            keep_c(b - 1, 0)
                    if b - 1 < PICK_END:
                        wait_added(At(b - 2))
                        copy_half(name, At(b - 1))
                    else:
                        late_half(At(b - 1))
                    if b - 2 < PICK_END:
                        wait_added(At(b - 2))
                        gelu(At(b - 2))
                    else:
                        late_gelu(At(b - 2))

                def late(b):
                    splits(b)
                    late_half(b.plus(-1))
                    late_gelu(b.plus(-2))

                def scores_out():
                    for n in range(8):
                        act.wait_ge(sem(f"score_ps{layer}"), n + 1)
                        nc.scalar.activation(
                            scores[:, 4 * n:4 * n + 4, :].rearrange("p s n -> p (s n)"),
                            ps[:, 2 + n % 2, :], ACT.Copy).then_inc(sem(f"scores{layer}"), 1)

                split_hi(At(base[name] + 1))
                splits(At(1))
                copy_half(name, At(0))
                scores_out()
                nc.scalar.preload_act_table(ACT.Gelu)
                repeat(act, 2, GATE_STEP, 2, early)
                act.wait_ge(sem(f"shifted{layer}"), 1)
                nc.scalar.activation(picked[:, :, 2, :],
                                     shifted.rearrange("p m h k -> p m (h k)"),
                                     ACT.Exp).then_inc(sem(f"gate_exp{layer}"), 1)
                nc.scalar.preload_act_table(ACT.Gelu)
                repeat(act, GATE_STEP, PICK_END, 2, early)
                act.wait_ge(sem(f"picks_ps{layer}"), 1)
                for m in range(2):
                    last = nc.scalar.activation(
                        picks[:, :, m * P:(m + 1) * P],
                        ps[:, 2 + m, 0:384].rearrange("p (w t) -> p w t", w=3), ACT.Copy)
                last.then_inc(sem(f"picks_T{layer}"), 1)
                for b in range(PICK_END, CUT + 2):
                    building(b)
                repeat(act, CUT + 2, P, 2, late)
                split_hi(At(base[f"v{layer}"]))
                for s in range(2):
                    act.wait_ge(group_out[s], GROUPS // 2 * (layer + 1))
                h_hi(layer, At(0))
                late_half(At(P - 1))
                late_gelu(At(P - 2))
                split_hi(At(base[f"v{layer}"] + 1))
                late_gelu(At(P - 1))

            def x_hi(k):
                for g in range(8):
                    m, q = divmod(g, 4)
                    act.wait_ge(sem(f"xt_ps{k}"), g + 1)
                    nc.scalar.activation(
                        xT[:, 4 * q:4 * q + 4, 0, m * P:(m + 1) * P],
                        ps[:, 2 + g % TURN_BANKS, :].rearrange("p (c t) -> p c t", c=4),
                        ACT.Copy).then_inc(sem(f"xt_hi{k}"), 1)

            def ln_std(k, following=None):
                nc.scalar.preload_act_table(ACT.Sqrt)
                act.wait_ge(sem("eps_set"), 1)
                for m in range(2):
                    act.wait_ge(sem(f"ln_mean{k}"), m + 1)
                    for c in range(4 if m == 0 else 0):
                        part = slice(512 * c, 512 * c + 512)
                        nc.scalar.activation(centred[:, part], residual[:, 0, part], ACT.Identity,
                                             bias=neg_mean[:, 0:1]).then_inc(
                                                 sem(f"ln_centred{k}"), 1)
                    nc.scalar.activation(deviation, residual[:, m, :], ACT.Square,
                                         bias=neg_mean[:, m:m + 1],
                                         accum_out=var_sum[:, m:m + 1]).then_inc(
                                             sem(f"ln_var{k}"), 1)
                    act.wait_ge(sem(f"ln_var{k}"), m + 1)
                    nc.scalar.activation(rstd[:, m:m + 1], var_sum[:, m:m + 1], ACT.Sqrt,
                                         scale=1.0 / D, bias=ln_eps).then_inc(
                                             sem(f"ln_std{k}"), 1)
                    if following:
                        split_hi(At(base[following] + m))

            def square_latents():
                b22 = first_block["even_in"] + n_blocks("even_in") - 1
                act.wait_ge(bank_free[b22 % 2], b22 // 2 + 1)
                act.wait_ge(bank_free[(b22 - 1) % 2], (b22 - 1) // 2 + 1)
                nc.scalar.activation(squares, blocks(CQ_AT, 6), ACT.Square).then_inc(sem("sq"), 1)

            def root_latents():
                act.wait_ge(sem("sq_ps"), 1)
                act.wait_ge(sem("eps_set"), 1)
                nc.scalar.activation(rms[:, 0, :], ps[:, 6, 0:T], ACT.Sqrt, bias=rms_eps,
                                     scale=1.0 / Q_LORA)
                nc.scalar.activation(rms[:, 1, :], ps[:, 6, T:2 * T], ACT.Sqrt, bias=rms_eps,
                                     scale=1.0 / KV_LORA).then_inc(sem("rms_std"), 1)

            def latent_out(n):
                act.wait_ge(sem("mla_ps"), n + 1)
                if n < 10:
                    dst = blocks((QB if n < 6 else KN - 12) + 2 * n, 2)
                else:
                    m, c = divmod(n - 10, 2)
                    dst = val_b[:, m, 512 * c:512 * c + 512]
                nc.scalar.activation(dst, ps[:, 6 + n % 2, :], ACT.Copy).then_inc(sem("mla_out"), 1)

            def soft_exp(h):
                act.wait_ge(sem("max_ready"), h + 1)
                for m in range(2):
                    e = probs[:, h % 4, 128 * m:128 + 256 * m]
                    kw = {"accum_out": row_sum[:, h, m:m + 1]} if h >= HEADS else {}
                    last = nc.scalar.activation(e, e, ACT.Exp, bias=neg_max[:, h, m:m + 1], **kw)
                last.then_inc(sem("exp_ready"), 1)

            def probs_out(h):
                act.wait_ge(sem("turned_ps"), h + 1)
                if h >= 2:
                    act.wait_ge(sem("head_ps0"), h - 1)
                nc.scalar.activation(probs_t[:, h % 2, :], ps[:, 4 + h % 2, 0:384],
                                     ACT.Copy).then_inc(sem("turned"), 1)

            def head_hi(layer, h):
                act.wait_ge(sem(f"head_ps{layer}"), h + 1)
                nc.scalar.activation(xT[:, h, 0, :], ps[:, h % 2, 0:T], ACT.Copy).then_inc(
                    sem(f"heads_hi{layer}"), 1)

            def head_hi0(h):
                head_hi(0, h)

            def head_hi1(h):
                head_hi(1, h)

            def stick_exp(h):
                act.wait_ge(sem("z_kept"), h + 1)
                if h >= 2:
                    act.wait_ge(sem("log_ready"), h - 1)
                nc.scalar.activation(z_abs[:, h % 2, :], z_kept[:, h % 6, :], ACT.Abs).then_inc(sem("abs_ready"), 1)
                act.wait_ge(sem("abs_ready"), h + 1)
                nc.scalar.activation(z_exp[:, h % 2, :], z_abs[:, h % 2, :], ACT.Exp,
                                     scale=-1.0).then_inc(sem("zexp_ready"), 1)

            def stick_log(h):
                act.wait_ge(sem("zexp_ready"), h + 1)
                if h >= 2:
                    act.wait_ge(sem("rest_ready"), h - 1)
                nc.scalar.activation(z_log[:, h % 2, :], z_exp[:, h % 2, :], ACT.Ln,
                                     bias=1.0).then_inc(sem("log_ready"), 1)

            def stick_att(h):
                act.wait_ge(sem("sum_ready"), h + 1)
                nc.scalar.activation(att[:, h % 2, :], att[:, h % 2, :], ACT.Exp).then_inc(
                    sem("att_ready"), 1)

            def values(layer):
                name = f"v{layer}"

                def row(b):
                    split_hi(b.times(2).plus(base[name]))
                    split_hi(b.times(2).plus(base[name] + 1))
                    h_hi(layer, b.plus(1))

                h_hi(layer, At(1))
                for s in range(2):
                    act.wait_ge(half_free[s], (P - PICK_END) // 2 * (layer + 1))
                repeat(act, 1, P - 1, 2, row)
                token_splits(name, 2 * P - 2)

            split_hi(At(0))
            split_hi(At(1))
            x_hi(0)
            feature("even_in", "even_v")
            token_splits("even_v", 1, 3)
            square_latents()
            token_splits("even_v", 3, 6)
            root_latents()
            token_splits("even_v", 6)
            act.wait_ge(sem("va_ps"), 1)
            for c in range(2):
                last = nc.scalar.activation(val_a[:, 0, 512 * c:512 * c + 512], ps[:, 2 + c, :],
                                            ACT.Copy)
            last.then_inc(sem("va_out0"), 1)
            for k in range(SOFT_STEPS):
                if k < 7:
                    latent_out(2 * k)
                    latent_out(2 * k + 1)
                if k in (3, 4):
                    split_hi(At(base["even_out"] + k - 3))
                for part, h in beside(k, ((soft_exp, 2), (probs_out, 5), (head_hi0, 7)), 2 * HEADS):
                    part(h)
            token_splits("even_out", 2)
            ln_std(0, "query0")
            x_hi(1)
            for layer in range(2):
                feature(f"query{layer}", f"u{layer}")
                experts(layer)
                values(layer)
                ln_std(2 * layer + 1, "odd_in" if layer == 0 else None)
                if layer == 0:
                    x_hi(2)
                    feature("odd_in", "odd_v")
                    token_splits("odd_v", 1)
                    act.wait_ge(sem("vc_ps"), 1)
                    for m in range(2):
                        for c in range(2):
                            nc.scalar.activation(val_c[:, m, 512 * c:512 * c + 512],
                                                 ps[:, column_bank(m, c), :], ACT.Copy).then_inc(
                                                     sem("vc_out"), 1)
                    nc.scalar.preload_act_table_set("natural_log_exp_and_others")
                    for k in range(STICK_STEPS):
                        if k in (3, 4):
                            split_hi(At(base["odd_out"] + k - 3))
                        for part, h in beside(k, ((head_hi1, 8), (stick_att, 6), (stick_log, 2),
                                                   (stick_exp, 1)), C_HEADS):
                            part(h)
                    token_splits("odd_out", 2)
                    ln_std(2, "query1")
                    x_hi(3)

        @block.vector
        def _(dve):
            count = [0]

            def settle(ins):
                count[0] += 1
                ins.then_inc(sem("dve_steps"), 1)
                dve.wait_ge(sem("dve_steps"), count[0])

            def half_lo(g, q):
                h = g.times(2).plus(q)
                dve.wait_ge(hi_ready[h.slot(SPLITS)], h.turn(SPLITS, 1))
                nc.vector.tensor_tensor(w_lo[:, h.slot(SPLITS), :],
                                        stage[:, g.slot(STAGES), HALF * q:HALF * q + HALF],
                                        w_hi[:, h.slot(SPLITS), :].bitcast(F32),
                                        ALU.subtract).then_inc(lo_ready[h.slot(SPLITS)], 1)

            def split_lo(g):
                for q in range(2):
                    half_lo(g, q)

            def token_splits(name, first=0, last=None):
                last = t[name].shape[0] if last is None else last
                repeat(dve, base[name] + first, base[name] + last, STAGES, split_lo)

            def add_up(name, b, dest):
                k = b.plus(first_block[name])
                dve.wait_ge(half_ready[k.slot(2)], k.turn(2, 1))
                nc.vector.tensor_tensor(arena[:, b.plus(dest).index(), :], ps[:, k.slot(2), 0:T],
                                        half_sum[:, k.slot(2), :], ALU.add).then_inc(
                                            bank_free[k.slot(2)], 1)

            def feature(name, dest, following):
                n = n_blocks(name)

                def step(b):
                    split_lo(b.times(2).plus(base[name]))
                    split_lo(b.times(2).plus(base[name] + 1))
                    add_up(name, b.plus(-1), dest)

                repeat(dve, 1, n, 2, step)
                split_lo(At(base[following]))
                add_up(name, At(n - 1), dest)

            def mixer_in():
                name = "even_in"

                def step(b):
                    split_lo(b.times(2).plus(base[name]))
                    split_lo(b.times(2).plus(base[name] + 1))
                    add_up(name, b.plus(-1), RAW)

                def step_rotate(b):
                    split_lo(b.times(2).plus(base[name]))
                    split_lo(b.times(2).plus(base[name] + 1))
                    n = b.plus(-ROPE_FROM - 1)
                    x = arena[:, bass.ds(n.index(), 2), :]
                    cos, sin = (trig[:, k, :].unsqueeze(1).to_broadcast([P, 2, T])
                                for k in range(2))
                    y = rotated[:, 0, :].rearrange("p (b t) -> p b t", b=2)
                    dve.wait_ge(sem("rot_ps"), n.turn(2, 1))
                    nc.vector.tensor_tensor(
                        y, ps[:, 2, :].rearrange("p (b t) -> p b t", b=2), sin, ALU.mult)
                    nc.vector.tensor_tensor(x, x, cos, ALU.mult).then_inc(sem("rope_parts"), 1)
                    dve.wait_ge(sem("rope_parts"), n.turn(2, 1))
                    nc.vector.tensor_tensor(x, x, y, ALU.add)
                    add_up(name, b.plus(-1), RAW)

                def turn(n):
                    step_rotate(n.times(2).plus(ROPE_FROM + 1))
                    step(n.times(2).plus(ROPE_FROM + 2))

                for b in range(1, ROPE_FROM + 1):
                    step(At(b))
                dve.wait_ge(sem("rot_in"), 32)
                repeat(dve, 0, HEADS, 1, turn)
                for b in range(ROPE_FROM + 2 * HEADS + 1, n_blocks(name)):
                    step(At(b))
                split_lo(At(base["even_v"]))
                add_up(name, At(n_blocks(name) - 1), RAW)

            def all_added(name):
                for b in (n_blocks(name) - 2, n_blocks(name) - 1):
                    k = At(b + first_block[name])
                    dve.wait_ge(bank_free[k.slot(2)], k.turn(2, 1))

            def x_lo(k, g):
                m, q = divmod(g, 4)
                dve.wait_ge(sem(f"xt_hi{k}"), g + 1)
                nc.vector.tensor_tensor(
                    xT[:, 4 * q:4 * q + 4, 1, m * P:(m + 1) * P],
                    ps[:, 2 + g % TURN_BANKS, :].rearrange("p (c t) -> p c t", c=4),
                    xT[:, 4 * q:4 * q + 4, 0, m * P:(m + 1) * P].bitcast(F32),
                    ALU.subtract).then_inc(sem(f"xt_lo{k}"), 1)

            def normed(k, m, c):
                part = slice(512 * c, 512 * c + 512)
                if m == 0:
                    dve.wait_ge(sem(f"ln_scaled{k}"), c + 1)
                nc.vector.scalar_tensor_tensor(
                    out=residual[:, m, part], in0=scaled[:, m, part], scalar=rstd[:, m:m + 1],
                    in1=bias[:, part], op0=ALU.mult, op1=ALU.add).then_inc(sem(f"ln_out{k}"), 1)

            def layer_norm(k, name, following=None):
                dve.wait_ge(sem(f"ln_in{k}"), 4 * 16)
                for m in range(2):
                    for c in range(4):
                        if m == 0:
                            dve.wait_ge(sem(f"y_ps{k}"), c + 1)
                        else:
                            h = At(2 * (base[name] + t[name].shape[0]) - 4 + c)
                            dve.wait_ge(used[h.slot(SPLITS)], h.turn(SPLITS, 1))
                        part = residual[:, m, 512 * c:512 * c + 512]
                        last = nc.vector.scalar_tensor_tensor(
                            out=part, in0=part, scalar=ALPHA, in1=ps[:, column_bank(m, c), :],
                            op0=ALU.mult, op1=ALU.add, accum_out=sums[:, m, c:c + 1])
                    settle(last)
                    settle(nc.vector.tensor_reduce(total[:, m:m + 1], sums[:, m, :], AX.X,
                                                   ALU.add))
                    nc.vector.tensor_scalar(neg_mean[:, m:m + 1], total[:, m:m + 1], -1.0 / D,
                                            None, ALU.mult).then_inc(sem(f"ln_mean{k}"), 1)

                dve.wait_ge(sem(f"ln_mean{k}"), 2)
                settle(nc.vector.scalar_tensor_tensor(
                    out=scaled[:, 1, :], in0=residual[:, 1, :], scalar=neg_mean[:, 1:2], in1=gain,
                    op0=ALU.add, op1=ALU.mult))

                def inverse(m):
                    dve.wait_ge(sem(f"ln_std{k}"), m + 1)
                    settle(nc.vector.reciprocal(rstd[:, m:m + 1], rstd[:, m:m + 1]))

                inverse(0)
                for c in range(4):
                    normed(k, 0, c)
                if following:
                    x_lo(k + 1, 0)
                    x_lo(k + 1, 1)
                inverse(1)
                for c in range(4):
                    normed(k, 1, c)
                    if following and c < 3:
                        x_lo(k + 1, 2 + c)
                if following:
                    split_lo(At(base[following]))
                    x_lo(k + 1, 5)
                    split_lo(At(base[following] + 1))
                    x_lo(k + 1, 6)
                    x_lo(k + 1, 7)

            def latent(n):
                if n == 0:
                    dve.wait_ge(sem("mla_in"), 16 * 9)
                    dve.wait_ge(sem("rms_std"), 1)
                    settle(nc.vector.reciprocal(rms, rms))
                for j in (2 * n, 2 * n + 1):
                    src, dst, g = ((CQ_AT + j, CQN + j, q_gain[:, j:j + 1]) if j < 4 else
                                   (CKV_AT + j - 4, CKVN + j - 4, kv_gain[:, j - 4:j - 3]))
                    last = nc.vector.scalar_tensor_tensor(
                        out=arena[:, dst, :], in0=arena[:, src, :], scalar=g,
                        in1=rms[:, j // 4, :], op0=ALU.mult, op1=ALU.mult)
                last.then_inc(sem("latents"), 1)

            def rotate(n, at, count, which):
                x = arena[:, at:at + count, :]
                cos, sin = (trig[:, 2 * which + k, :].unsqueeze(1).to_broadcast([P, count, T])
                            for k in range(2))
                y = (rotated if n == HEADS else rotated_b)[:, n % 2, 0:count * T].rearrange(
                    "p (b t) -> p b t", b=count)
                dve.wait_ge(sem("rot_ps"), n + 1)
                nc.vector.tensor_tensor(
                    y, ps[:, rotate_bank(n), 0:count * T].rearrange("p (b t) -> p b t", b=count), sin,
                    ALU.mult)
                settle(nc.vector.tensor_tensor(x, x, cos, ALU.mult))
                nc.vector.tensor_tensor(x, x, y, ALU.add).then_inc(sem("roped"), 1)

            def soft_max(h):
                dve.wait_ge(sem("logit_ps"), h + 1)
                if h >= 4:
                    dve.wait_ge(sem("turned_ps"), h - 3)
                mask = even_masks[:, 1 if h < HEADS else 2, :]
                settle(nc.vector.scalar_tensor_tensor(
                    out=probs[:, h % 4, :], in0=ps[:, 2 + h % 2, 0:384],
                    scalar=A_SCALE if h < HEADS else B_SCALE, in1=mask, op0=ALU.mult, op1=ALU.add))
                for m in range(2):
                    last = nc.vector.tensor_reduce(neg_max[:, h, m:m + 1],
                                                   probs[:, h % 4, 128 * m:128 + 256 * m],
                                                   AX.X, ALU.max, negate=True)
                last.then_inc(sem("max_ready"), 1)

            def soft_norm(h):
                dve.wait_ge(sem("exp_ready"), h + 1)
                tiles = [probs[:, h % 4, 128 * m:128 + 256 * m] for m in range(2)]
                if h < HEADS:
                    for m in range(2):
                        last = nc.vector.tensor_tensor_reduce(
                            out=tiles[m], in0=tiles[m],
                            in1=even_masks[:, 0, 128 * m:128 + 256 * m], scale=1.0, scalar=0.0,
                            op0=ALU.mult, op1=ALU.add, accum_out=row_sum[:, h, m:m + 1])
                    settle(last)
                settle(nc.vector.reciprocal(inv_sum[:, h, :], row_sum[:, h, :]))
                for m in range(2):
                    last = nc.vector.tensor_scalar(tiles[m], tiles[m], inv_sum[:, h, m:m + 1], None,
                                                   ALU.mult)
                last.then_inc(sem("probs_ready"), 1)

            def head_lo(layer, h):
                dve.wait_ge(sem(f"heads_hi{layer}"), h + 1)
                nc.vector.tensor_tensor(xT[:, h, 1, :], ps[:, h % 2, 0:T],
                                        xT[:, h, 0, :].bitcast(F32), ALU.subtract).then_inc(
                                            sem(f"heads_lo{layer}"), 1)

            def head_lo0(h):
                head_lo(0, h)

            def head_lo1(h):
                head_lo(1, h)

            def stick_rest(h):
                dve.wait_ge(sem("log_ready"), h + 1)
                dve.wait_ge(sem("z_kept"), h + 1)
                if h >= 2:
                    dve.wait_ge(sem("suffix_ps"), h - 1)
                nc.vector.scalar_tensor_tensor(
                    out=rest[:, h % 2, :], in0=z_kept[:, h % 6, :], scalar=0.0,
                    in1=z_log[:, h % 2, :], op0=ALU.max, op1=ALU.add).then_inc(
                        sem("rest_ready"), 1)

            def stick_keep(h):
                dve.wait_ge(sem("z_ps"), h + 1)
                nc.vector.tensor_copy(z_kept[:, h % 6, :], ps[:, Z_BANKS[h % 4], 0:384]).then_inc(
                    sem("z_kept"), 1)

            def stick_sum(h):
                dve.wait_ge(sem("suffix_ps"), h + 1)
                if h >= 2:
                    dve.wait_ge(sem("head_ps1"), h - 1)
                nc.vector.tensor_tensor(att[:, h % 2, :], z_kept[:, h % 6, :],
                                        ps[:, 4 + h % 2, 0:384], ALU.add).then_inc(
                                            sem("sum_ready"), 1)

            def top16(values, cut, v, i, rows):
                for s in rows:
                    last = nc.vector.max(v(s)[:, 0:8], values[:, s, :])
                settle(last)
                for s in rows:
                    nc.vector.max_index(i(s)[:, 0:8], v(s)[:, 0:8], values[:, s, :])
                    last = nc.vector.match_replace(cut[:, s, :], v(s)[:, 0:8], values[:, s, :],
                                                   REPLACED)
                settle(last)
                for s in rows:
                    last = nc.vector.max(v(s)[:, 8:16], cut[:, s, :])
                settle(last)
                for s in rows:
                    last = nc.vector.max_index(i(s)[:, 8:16], v(s)[:, 8:16], cut[:, s, :])
                return last

            def pick(layer, n):
                if n == 0:
                    dve.wait_ge(sem(f"scores{layer}"), 8)
                if n < 16:
                    settle(top16(scores, scores_cut, lambda s: top_v[:, s, :],
                                 lambda s: top_i[:, s, :], (2 * n, 2 * n + 1)))
                elif n < 33:
                    if n == 16:
                        nc.vector.tensor_copy(top_f, top_i.rearrange("p s k -> p (s k)"))
                    if n < 20:
                        m, first = divmod(4 * (n - 16), HEADS)
                        sides = top_v.rearrange("p (m h two) k -> p m h two k", m=2, two=2)[
                            :, m, first:first + 4]
                        last = nc.vector.tensor_tensor(
                            cand[:, 4 * (n - 16):4 * (n - 16) + 4, :].rearrange(
                                "p h (a b) -> p h a b", a=TOPK),
                            sides[:, :, 0, :].unsqueeze(3).to_broadcast([P, 4, TOPK, TOPK]),
                            sides[:, :, 1, :].unsqueeze(2).to_broadcast([P, 4, TOPK, TOPK]),
                            ALU.add)
                    if n > 16:
                        last = top16(cand, cand_cut, lambda s: best_v[:, s, :],
                                     lambda s: best_i[:, TOPK * s:TOPK * s + TOPK], (n - 17,))
                    settle(last)
                elif n == 33:
                    nc.vector.tensor_tensor(
                        shifted.rearrange("p m h k -> p (m h) k"), best_v,
                        best_v[:, :, 0:1].to_broadcast([P, 2 * HEADS, TOPK]),
                        ALU.subtract).then_inc(sem(f"shifted{layer}"), 1)
                    nc.vector.tensor_scalar(rank_i[:, 0, :], best_i, 4, None,
                                            ALU.logical_shift_right)
                    settle(nc.vector.tensor_scalar(rank_i[:, 1, :], best_i, 15, None,
                                                   ALU.bitwise_and))
                    settle(nc.vector.tensor_copy(
                        rank_f.rearrange("p s m n -> p (s m n)"),
                        rank_i.rearrange("p s n -> p (s n)")))
                else:
                    turn, stage_n = divmod(n - 34, 3)
                    m, side = divmod(turn, 2)
                    eq = match.rearrange("p (n a) -> p n a", a=TOPK)
                    by_head = match.rearrange("p (h k a) -> p h k a", h=HEADS, k=TOPK)
                    keys = top_f.rearrange("p (m h two k) -> p m h two k", m=2, h=HEADS, two=2)
                    if stage_n == 0:
                        settle(nc.vector.tensor_tensor(
                            eq, iota[:, 0:TOPK].unsqueeze(1).to_broadcast([P, P, TOPK]),
                            rank_f[:, side, m, :].unsqueeze(2).to_broadcast([P, P, TOPK]),
                            ALU.is_equal))
                    elif stage_n == 1:
                        settle(nc.vector.tensor_tensor(
                            by_head, by_head, keys[:, m, :, side, :].unsqueeze(2).to_broadcast(
                                [P, HEADS, TOPK, TOPK]), ALU.mult))
                    else:
                        settle(nc.vector.tensor_reduce(picked[:, m, side, :], eq, AX.X, ALU.add))
                if n == PICK_PARTS - 1:
                    dve.wait_ge(sem(f"gate_exp{layer}"), 1)
                    for m in range(2):
                        last = nc.vector.tensor_reduce(
                            gate_sum[:, m, :], picked[:, m, 2, :].rearrange(
                                "p (h k) -> p h k", h=HEADS), AX.X, ALU.add)
                    settle(last)
                    settle(nc.vector.reciprocal(gate_inv, gate_sum))
                    for m in range(2):
                        g = picked[:, m, 2, :].rearrange("p (h k) -> p h k", h=HEADS)
                        last = nc.vector.tensor_tensor(
                            g, g, gate_inv[:, m, :].unsqueeze(2).to_broadcast([P, HEADS, TOPK]),
                            ALU.mult)
                    last.then_inc(sem(f"picks_done{layer}"), 1)

            def h_lo(layer, b):
                dve.wait_ge(sem(f"h_hi{layer}"), b.turn(1, 1))
                nc.vector.tensor_tensor(xT[:, b.slot(2), 1, :], arena[:, b.index(), :],
                                        xT[:, b.slot(2), 0, :].bitcast(F32),
                                        ALU.subtract).then_inc(sem(f"h_lo{layer}"), 1)

            def experts(layer):
                name = f"u{layer}"

                def splits(b):
                    split_lo(b.times(2).plus(base[name]))
                    split_lo(b.times(2).plus(base[name] + 1))

                def hots(g):
                    k = group_at(layer, At(g))
                    wait_round(dve, group_ps[k.slot(2)], k.turn(2))
                    for side, hot in ((0, hot1), (1, hot2)):
                        chosen = picks[:, side, GROUP * g:GROUP * g + GROUP].unsqueeze(2)
                        last = nc.vector.tensor_tensor(
                            hot[:, k.slot(2), :, :],
                            iota.unsqueeze(1).to_broadcast([P, GROUP, P]),
                            chosen.to_broadcast([P, GROUP, P]), ALU.is_equal)
                    last.then_inc(hots_equal[k.slot(2)], 1)

                def gate(b, j):
                    g = BUILD * (b - PICK_END) + j
                    k = group_at(layer, At(g))
                    dve.wait_ge(group_kept[k.slot(2)], k.turn(2, 1))
                    dve.wait_ge(sem(f"gelu{layer}"), b)
                    h = by_group[:, 0:b, g, :]
                    c = ps[:, 2 + k.slot(GROUP_BANKS), :].rearrange("p (t i) -> p i t", t=GROUP)
                    nc.vector.tensor_tensor(h, c[:, 0:b, :], h, ALU.mult).then_inc(
                        group_out[k.slot(2)], 1)

                def late_add(b):
                    k = b.plus(first_block[name])
                    dve.wait_ge(half_ready[k.slot(2)], k.turn(2, 1))
                    nc.vector.tensor_tensor(half_sum[:, k.slot(2), :], ps[:, k.slot(2), 0:T],
                                            half_sum[:, k.slot(2), :], ALU.add).then_inc(
                                                bank_free[k.slot(2)], 1)

                def late_gate(b):
                    k = b.plus(first_block[name])
                    first = T if b.i is not None else built_before(b.c)
                    dve.wait_ge(sem(f"gelu{layer}"), b.turn(1, 1))
                    nc.vector.tensor_tensor(arena[:, b.index(), 0:first],
                                            arena[:, b.index(), 0:first],
                                            half_sum[:, k.slot(2), 0:first], ALU.mult).then_inc(
                                                half_free[b.slot(2)], 1)

                def building(b):
                    for q in range(4):
                        half_lo(At(2 * b + base[name] + q // 2), q % 2)
                        if q == 0 and b - 3 >= PICK_END:
                            late_gate(At(b - 3))
                        if q % 2 == 0 and PICK_END <= b - 2 < CUT:
                            gate(b - 2, q // 2)
                        if q % 2 == 1 and b < CUT:
                            hots(BUILD * (b - PICK_END) + q // 2)
                    if b - 1 < PICK_END:
                        add_up(name, At(b - 1), 0)
                    else:
                        late_add(At(b - 1))

                def late(b):
                    splits(b)
                    late_gate(b.plus(-3))
                    late_add(b.plus(-1))

                split_lo(At(base[name] + 1))
                for b in range(1, PICK_END):
                    splits(At(b))
                    add_up(name, At(b - 1), 0)
                    if b <= PICK_PARTS:
                        pick(layer, b - 1)
                dve.wait_ge(sem(f"picks_T{layer}"), 1)
                for b in range(PICK_END, CUT + 2):
                    building(b)
                late(At(CUT + 2))
                repeat(dve, CUT + 3, P, 2, late)
                split_lo(At(base[f"v{layer}"]))
                h_lo(layer, At(0))
                late_gate(At(P - 3))
                late_add(At(P - 1))
                late_gate(At(P - 2))
                split_lo(At(base[f"v{layer}"] + 1))
                late_gate(At(P - 1))

            def values(layer):
                name = f"v{layer}"

                def row(b):
                    split_lo(b.times(2).plus(base[name]))
                    split_lo(b.times(2).plus(base[name] + 1))
                    h_lo(layer, b.plus(1))

                h_lo(layer, At(1))
                repeat(dve, 1, P - 1, 2, row)
                token_splits(name, 2 * P - 2)

            nc.vector.memset(ln_eps, LN_EPS)
            nc.vector.memset(rms_eps, RMS_EPS).then_inc(sem("eps_set"), 1)
            for g in range(8):
                x_lo(0, g)
                if g in (3, 5):
                    split_lo(At(g // 4))
            mixer_in()
            all_added("even_in")
            token_splits("even_v", 1, 4)
            rotate(HEADS, KR_AT, 1, 1)
            token_splits("even_v", 4, 8)
            for n in range(3):
                latent(n)
                token_splits("even_v", 8 + n, 9 + n)
            token_splits("even_v", 11)
            dve.wait_ge(sem("va_ps"), 1)
            for c in range(2):
                last = nc.vector.tensor_copy(val_a[:, 1, 512 * c:512 * c + 512], ps[:, 4 + c, :])
            last.then_inc(sem("va_out1"), 1)
            for k in range(SOFT_STEPS):
                for part, h in beside(k, ((soft_max, 1), (soft_norm, 3), (head_lo0, 7)), 2 * HEADS):
                    part(h)
                if k in (3, 4):
                    split_lo(At(base["even_out"] + k - 3))
                if k == 7:
                    for n in range(2):
                        rotate(9 + n, QB + 8 + 2 * n, 2, 1)
            token_splits("even_out", 2)
            layer_norm(0, "even_out", "query0")
            for layer in range(2):
                feature(f"query{layer}", QT_AT, f"u{layer}")
                dve.wait_ge(sem(f"kept{2 * layer}"), 16)
                experts(layer)
                values(layer)
                layer_norm(2 * layer + 1, f"v{layer}", "odd_in" if layer == 0 else None)
                if layer == 0:
                    dve.wait_ge(sem("kept1"), 16)
                    feature("odd_in", OQ_AT, "odd_v")
                    all_added("odd_in")
                    q = blocks(OQ_AT, 16)
                    nc.vector.tensor_scalar(q, q, A_SCALE, None, ALU.mult).then_inc(
                        sem("q_scaled"), 1)
                    token_splits("odd_v", 1)
                    dve.wait_ge(sem("vc_ps"), 1)
                    for m in (1, 0):
                        for c in (2, 3):
                            nc.vector.tensor_copy(val_c[:, m, 512 * c:512 * c + 512],
                                                  ps[:, column_bank(m, c), :]).then_inc(
                                                      sem("vc_out_high"), 1)
                    for k in range(STICK_STEPS):
                        if k in (3, 4):
                            split_lo(At(base["odd_out"] + k - 3))
                        for part, h in beside(k, ((stick_keep, 1), (stick_rest, 3), (stick_sum, 5),
                                                   (head_lo1, 8)), C_HEADS):
                            part(h)
                    token_splits("odd_out", 2)
                    layer_norm(2, "odd_out", "query1")

        @block.tensor
        def _(pe):
            def mm(out, lhs, rhs, start, stop):
                return nc.tensor.matmul(out, lhs, rhs, start=start, stop=stop)

            def turn_x(k, source, ready):
                for g in range(8):
                    m, q = divmod(g, 4)
                    if k:
                        pe.wait_ge(sem(ready), g + 1)
                    elif g % 2 == 0:
                        pe.wait_ge(sem(f"{ready}{g // 2}"), 16)
                    if g >= TURN_BANKS:
                        pe.wait_ge(sem(f"xt_lo{k}"), g - TURN_BANKS + 1)
                    for c in range(4):
                        last = nc.tensor.transpose(
                            ps[:, 2 + g % TURN_BANKS, P * c:P * c + P],
                            source[:, m, (4 * q + c) * P:(4 * q + c + 1) * P], ident)
                    last.then_inc(sem(f"xt_ps{k}"), 1)

            def feature_block(name, b, x=None, behind=None):
                k = b.plus(first_block[name])
                bank = ps[:, k.slot(2), :]
                wait_round(pe, bank_free[k.slot(2)], k.turn(2))
                for q in range(4):
                    if x is not None:
                        pe.wait_ge(sem(f"xt_lo{x}"), 5 + q)
                    h = b.times(4).plus(2 * base[name] + q)
                    pe.wait_ge(lo_ready[h.slot(SPLITS)], h.turn(SPLITS, 1))
                    hi = w_hi[:, h.slot(SPLITS), :].rearrange("p (k n) -> p k n", k=4)
                    lo = w_lo[:, h.slot(SPLITS), :].rearrange("p (k n) -> p k n", k=4)
                    for c in range(4):
                        kc = 4 * q + c
                        both = xT[:, kc, :, :].rearrange("p s t -> p (s t)")
                        if kc < KC - 1:
                            mm(bank, hi[:, c, :], both, kc == 0, False)
                            last = mm(bank[:, 0:T], lo[:, c, :], xT[:, kc, 0, :], False, False)
                        else:
                            mm(bank[:, 0:T], lo[:, c, :], xT[:, kc, 0, :], False, False)
                            last = mm(bank, hi[:, c, :], both, False, True)
                    last.then_inc(used[h.slot(SPLITS)], 1)
                    if behind:
                        behind(q)

            def feature(name, x):
                feature_block(name, At(0), x)
                repeat(pe, 1, n_blocks(name), 2, lambda b: feature_block(name, b))

            def mixer_in():
                def turn(n):
                    here = n.times(2)
                    feature_block("even_in", here.plus(ROPE_FROM))
                    mm(ps[:, 2, :], rot_a,
                       arena[:, bass.ds(here.index(), 2), :].rearrange("p b t -> p (b t)"),
                       True, True).then_inc(sem("rot_ps"), 1)
                    feature_block("even_in", here.plus(ROPE_FROM + 1))

                feature_block("even_in", At(0), 0)
                for b in range(1, ROPE_FROM):
                    feature_block("even_in", At(b))
                pe.wait_ge(sem("rot_in"), 32)
                repeat(pe, 0, HEADS, 1, turn)
                for b in range(ROPE_FROM + 2 * HEADS, n_blocks("even_in")):
                    feature_block("even_in", At(b))

            def token_unit(g, lhs, banks, start, stop):
                for c in range(2):
                    h = g.times(2).plus(c)
                    pe.wait_ge(lo_ready[h.slot(SPLITS)], h.turn(SPLITS, 1))
                    hi, lo = w_hi[:, h.slot(SPLITS), :], w_lo[:, h.slot(SPLITS), :]
                    for m in range(2):
                        xh, xl = (lhs[:, s, m * P:(m + 1) * P] for s in range(2))
                        out = ps[:, banks[m] + c, :]
                        mm(out, xh, hi, start, False)
                        mm(out, xh, lo, False, False)
                        last = mm(out, xl, hi, False, stop)
                    last.then_inc(used[h.slot(SPLITS)], 1)

            def last_row(gs, lhs, done):
                for m in range(2):
                    for q in range(4):
                        h = gs[q // 2].times(2).plus(q % 2)
                        pe.wait_ge(lo_ready[h.slot(SPLITS)], h.turn(SPLITS, 1))
                        hi, lo = w_hi[:, h.slot(SPLITS), :], w_lo[:, h.slot(SPLITS), :]
                        xh, xl = (lhs[:, s, m * P:(m + 1) * P] for s in range(2))
                        out = ps[:, column_bank(m, q), :]
                        mm(out, xh, hi, False, False)
                        mm(out, xh, lo, False, False)
                        last = mm(out, xl, hi, False, True)
                        last.then_inc(used[h.slot(SPLITS)] if m else sem(done), 1)

            def token(name, halves, between, done=None, begun=0):
                for kc in range(KC - 1 if done else KC):
                    for half in range(halves):
                        if kc == 0 and half < begun:
                            continue
                        between(kc, half)
                        g = At(base[name] + halves * kc + half)
                        banks = ([column_bank(m, 2 * half) for m in range(2)] if halves == 2 else
                                 [2, 4])
                        token_unit(g, xT[:, kc, :, :], banks, kc == 0, kc == KC - 1)
                if done:
                    last_row([At(base[name] + 2 * (KC - 1) + half) for half in range(2)],
                             xT[:, KC - 1, :, :], done)

            def all_read(name):
                end = first_block[name] + n_blocks(name)
                for s in range(2):
                    pe.wait_ge(bank_free[s], (end - s + 1) // 2)

            def token_done(name, done):
                h = At(2 * (base[name] + t[name].shape[0]) - 1)
                pe.wait_ge(used[h.slot(SPLITS)], h.turn(SPLITS, 1))
                pe.sem_inc(sem(done), 1)

            def sum_squares():
                pe.wait_ge(sem("sq"), 1)
                for k in range(4):
                    mm(ps[:, 6, 0:T], ones, squares[:, T * k:T * k + T], k == 0, k == 3)
                for k in range(2):
                    last = mm(ps[:, 6, T:2 * T], ones, squares[:, T * (4 + k):T * (5 + k)], k == 0,
                              k == 1)
                last.then_inc(sem("sq_ps"), 1)

            def latent_product(n):
                if n >= 2:
                    pe.wait_ge(sem("mla_out"), n - 1)
                else:
                    pe.wait_ge(sem("roped"), 1)
                    pe.wait_ge(sem("latents"), 3)
                bank = ps[:, 6 + n % 2, :]
                if n < 10:
                    w, kc, at = (w_qb, 4, CQN) if n < 6 else (w_kvb, 2, CKVN)
                    for j in range(2):
                        col = P * (2 * (n if n < 6 else n - 6) + j)
                        for k in range(kc):
                            last = mm(bank[:, T * j:T * j + T], w[:, k, col:col + P],
                                      arena[:, at + k, :], k == 0, k == kc - 1)
                else:
                    m, c = divmod(n - 10, 2)
                    for k in range(2):
                        last = mm(bank, arena[:, CKVN + k, m * P:(m + 1) * P],
                                  w_kvb[:, k, 1024 + 512 * c:1536 + 512 * c], k == 0, k == 1)
                last.then_inc(sem("mla_ps"), 1)

            def rotate(n, at, count, rot):
                mm(ps[:, rotate_bank(n), 0:count * T], rot, blocks(at, count), True, True).then_inc(
                    sem("rot_ps"), 1)

            def beside_values(kc, half):
                if kc == 3:
                    all_read("even_in")
                    rotate(HEADS, KR_AT, 1, rot_b)
                if kc == 5:
                    sum_squares()

            def begin_out(name, layer):
                pe.wait_ge(sem(f"heads_lo{layer}"), 1)
                token_unit(At(base[name]), xT[:, 0, :, :], [column_bank(m, 0) for m in range(2)],
                           True, False)

            def after_heads(layer):
                def wait(kc, half):
                    if half == 0:
                        pe.wait_ge(sem(f"heads_lo{layer}"), kc + 1)
                    elif kc == 0:
                        pe.wait_ge(sem(f"heads_lo{layer}"), 2 * HEADS)
                return wait

            def after_features(kc, half):
                if kc == 0 and half == 1:
                    all_read("odd_in")

            def logits(h):
                bank = ps[:, 2 + h % 2, :]
                if h >= 2:
                    pe.wait_ge(sem("max_ready"), h - 1)
                if h < HEADS:
                    parts = [(arena[:, Q_AT + h, :], arena[:, K_AT + h, :])]
                else:
                    j = h - HEADS
                    half = slice(ROPE * (j % 2), ROPE * (j % 2) + ROPE)
                    parts = [(arena[:, QB + j, :], arena[:, KN + j, :]),
                             (arena[half, QB + 8 + j // 2, :], arena[half, KR_AT, :])]
                for m in range(2):
                    out = bank[:, 128 * m:128 + 256 * m]
                    for n, (q, k) in enumerate(parts):
                        last = mm(out, q[:, m * P:(m + 1) * P], k[:, 0:P * (m + 1)], n == 0,
                                  n == len(parts) - 1)
                last.then_inc(sem("logit_ps"), 1)

            def turn_probs(h):
                pe.wait_ge(sem("probs_ready"), h + 1)
                if h >= 2:
                    pe.wait_ge(sem("turned"), h - 1)
                for b in range(3):
                    last = nc.tensor.transpose(ps[:, 4 + h % 2, P * b:P * b + P],
                                               probs[:, h % 4, P * b:P * b + P], ident)
                last.then_inc(sem("turned_ps"), 1)

            def head(layer, h, weights, ready, val, col):
                pe.wait_ge(sem(ready), h + 1)
                if h >= 2:
                    pe.wait_ge(sem(f"heads_lo{layer}"), h - 1)
                bank = ps[:, h % 2, :]
                mm(bank[:, 0:T], val[:, 0, col:col + P], weights[:, h % 2, 0:T], True, False)
                mm(bank[:, P:T], val[:, 1, col:col + P], weights[:, h % 2, T:384], False,
                   True).then_inc(sem(f"head_ps{layer}"), 1)

            def head_even(h):
                head(0, h, probs_t, "turned", val_a if h < HEADS else val_b, P * (h % HEADS))

            def head_odd(h):
                head(1, h, att, "att_ready", val_c, P * h)

            def stick_z(h):
                if h >= 4:
                    pe.wait_ge(sem("z_kept"), h - 3)
                else:
                    pe.wait_ge(sem("vc_out"), h + 1)
                bank = ps[:, Z_BANKS[h % 4], :]
                q, k = arena[:, OQ_AT + h, :], arena[:, OK_AT + h, :]
                mm(bank[:, 0:T], k[:, 0:P], q, True, False)
                mm(bank[:, 0:P], ident, diag_mask, False, True)
                mm(bank[:, T:384], k[:, P:T], q[:, P:T], True, False)
                mm(bank[:, T:384], ident, diag_mask, False, True).then_inc(sem("z_ps"), 1)

            def stick_suffix(h):
                pe.wait_ge(sem("rest_ready"), h + 1)
                if h >= 2:
                    pe.wait_ge(sem("sum_ready"), h - 1)
                else:
                    pe.wait_ge(sem("vc_out_high"), h + 1)
                bank, r = ps[:, 4 + h % 2, :], rest[:, h % 2, :]
                mm(bank[:, 0:T], neg_tri, r[:, 0:T], True, False)
                mm(bank[:, P:T], neg_ones, r[:, T:384], False, True)
                mm(bank[:, T:384], neg_tri, r[:, T:384], True, True).then_inc(
                    sem("suffix_ps"), 1)

            def score(layer):
                pe.wait_ge(sem(f"keys_in{layer}"), 16)
                for n in range(8):
                    if n >= 2:
                        pe.wait_ge(sem(f"scores{layer}"), n - 1)
                    m, g = divmod(n, 4)
                    for j in range(4):
                        s = 4 * g + j
                        last = mm(ps[:, 2 + n % 2, P * j:P * j + P],
                                  arena[:, QT_AT + s, m * P:(m + 1) * P], keys_t[:, s, :],
                                  True, True)
                    last.then_inc(sem(f"score_ps{layer}"), 1)

            def experts(layer):
                name = f"u{layer}"

                def one(b):
                    feature_block(name, b)

                def turn_picks():
                    pe.wait_ge(sem(f"picks_done{layer}"), 1)
                    for m in range(2):
                        for w in range(3):
                            last = nc.tensor.transpose(ps[:, 2 + m, P * w:P * w + P],
                                                       picked[:, m, w, :], ident)
                    last.then_inc(sem(f"picks_ps{layer}"), 1)

                def group(g):
                    k = group_at(layer, g)
                    wait_round(pe, group_out[k.slot(2)], k.turn(2, 1 - GROUP_BANKS // 2))
                    pe.wait_ge(hots_ready[k.slot(2)], k.turn(2, 1))
                    for j in range(GROUP):
                        last = mm(ps[:, 2 + k.slot(GROUP_BANKS), P * j:P * j + P],
                                  hot1[:, k.slot(2), j, :], hot2[:, k.slot(2), j, :], True, True)
                    last.then_inc(group_ps[k.slot(2)], 1)

                def building(n):
                    for r in range(2):
                        g = n.times(2 * BUILD).plus(BUILD * r)
                        feature_block(
                            name, n.times(2).plus(PICK_END + r),
                            behind=lambda q, g=g: group(g.plus(q // 2)) if q % 2 else None)

                one(At(0))
                all_read(f"query{layer}")
                score(layer)
                repeat(pe, 1, PICK_PARTS, 2, one)
                one(At(PICK_PARTS))
                turn_picks()
                one(At(PICK_PARTS + 1))
                repeat(pe, 0, (CUT - PICK_END) // 2, 1, building, peel=1)
                repeat(pe, CUT, P, 2, one)

            def values(layer):
                name = f"v{layer}"

                def row(b, start=False):
                    pe.wait_ge(sem(f"h_lo{layer}"), b.turn(1, 1))
                    for half in range(2):
                        if start and half == 1:
                            all_read(f"u{layer}")
                        token_unit(b.times(2).plus(base[name] + half), xT[:, b.slot(2), :, :],
                                   [column_bank(m, 2 * half) for m in range(2)], start, False)

                for s in range(2):
                    pe.wait_ge(group_out[s], GROUPS // 2 * (layer + 1))
                row(At(0), start=True)
                row(At(1))
                repeat(pe, 2, P - 2, 2, row)
                row(At(P - 2))
                pe.wait_ge(sem(f"h_lo{layer}"), P)
                last_row([At(base[name] + 2 * (P - 1) + half) for half in range(2)],
                         xT[:, (P - 1) % 2, :, :], f"y_ps{2 * layer + 1}")

            pe.wait_ge(sem("const_in"), 16)
            turn_x(0, x_first, "x_in")
            mixer_in()
            token("even_v", 1, beside_values)
            token_done("even_v", "va_ps")
            for k in range(SOFT_STEPS):
                if k < 7:
                    latent_product(2 * k)
                    latent_product(2 * k + 1)
                if k == 0:
                    pe.wait_ge(sem("va_out0"), 1)
                    pe.wait_ge(sem("va_out1"), 1)
                if k == 7:
                    pe.wait_ge(sem("mla_out"), 14)
                    for n in range(2):
                        rotate(9 + n, QB + 8 + 2 * n, 2, rot_b)
                if k == 8:
                    pe.wait_ge(sem("roped"), 3)
                if k == SOFT_STEPS - 4:
                    begin_out("even_out", 0)
                for part, h in beside(k, ((logits, 0), (turn_probs, 4), (head_even, 6)), 2 * HEADS):
                    part(h)
            token("even_out", 2, after_heads(0), "y_ps0", 1)
            turn_x(1, residual, "ln_out0")
            for layer in range(2):
                feature(f"query{layer}", 2 * layer + 1)
                experts(layer)
                values(layer)
                if layer == 0:
                    turn_x(2, residual, "ln_out1")
                    feature("odd_in", 2)
                    token("odd_v", 2, after_features)
                    token_done("odd_v", "vc_ps")
                    pe.wait_ge(sem("q_scaled"), 1)
                    pe.wait_ge(sem("odd_in"), 16)
                    for k in range(STICK_STEPS):
                        if k == 7:
                            pe.wait_ge(sem("vc_out_high"), 4)
                        if k == C_HEADS + 4:
                            begin_out("odd_out", 1)
                        for part, h in beside(k, ((stick_suffix, 4), (head_odd, 7), (stick_z, 0)),
                                               C_HEADS):
                            part(h)
                    token("odd_out", 2, after_heads(1), "y_ps2", 1)
                    turn_x(3, residual, "ln_out2")


def feature_units(w):
    n = w.shape[1] // P
    return np.ascontiguousarray(
        w.reshape(2, 8, P, n, P).transpose(3, 0, 2, 1, 4).reshape(2 * n, P, UNIT))


def token_units(w):
    n = w.shape[1] // UNIT
    return np.ascontiguousarray(w.reshape(KC, P, n, UNIT).transpose(0, 2, 1, 3).reshape(KC * n, P, UNIT))


def shape_constants():
    eye = np.eye(P, dtype=np.float32)
    iota = np.tile(np.arange(P, dtype=np.float32), (P, 1))
    ones = np.ones((P, P), np.float32)

    def rotation(half):
        r = np.zeros((P, P), np.float32)
        for m in range(P):
            low = m % (2 * half) < half
            r[m + half if low else m - half, m] = -1.0 if low else 1.0
        return r

    const = np.stack([eye, ones, iota], 1)
    rotations = np.stack([rotation(64), rotation(32)], 1)

    def angles(half):
        inv = np.float32(10000.0) ** (-np.arange(half, dtype=np.float32) / np.float32(half))
        ang = (np.arange(T, dtype=np.float32)[:, None] * inv[None, :]).astype(np.float32).T
        ang = np.tile(ang, (P // half, 1))
        return np.cos(ang).astype(np.float32), np.sin(ang).astype(np.float32)

    trig = np.stack([*angles(64), *angles(32)], 1)
    q, k = np.arange(T)[:, None], np.arange(T)[None, :]
    back = q - k
    count = (((back >= 0) & (back <= 128)).astype(np.float32) + ((back >= 0) & (back % 4 == 0))
             + ((back >= 0) & (back % 16 == 0)))

    def tiles(a):
        return np.concatenate([a[0:P, 0:P], a[P:T, 0:T]], 1)

    even_masks = np.stack([tiles(count), tiles(np.where(count > 0, 0.0, NEG)),
                           tiles(np.where(back >= 0, 0.0, NEG))], 1).astype(np.float32)
    j, s = np.arange(P)[:, None], np.arange(P)[None, :]
    neg_tri = -(j >= s).astype(np.float32)
    earlier = (j < s)
    diag = np.where(earlier, 0.0, NEG).astype(np.float32)
    odd_consts = np.concatenate([neg_tri, diag, -ones], 1)
    return {"const": const, "rotations": rotations, "trig": trig, "even_masks": even_masks, "odd_consts": odd_consts}


def layout(i):
    i = {k: np.asarray(v) for k, v in i.items()}
    w = i["a_w_in"][0]
    a, cq, ckv = 1024, 3072, 3584
    kr = w[:, 3840:3904]
    feats = np.concatenate([w[:, 0:2 * a], w[:, cq:ckv], w[:, ckv:3840], kr, kr], 1)
    wq = i["b_w_q_b"][0].reshape(4, P, HEADS, 192)
    wq = np.concatenate([wq[..., 0:P].reshape(4, P, 1024), wq[..., P:].reshape(4, P, 512)], 2)
    wkv = i["b_w_kv_b"][0].reshape(2, P, HEADS, 256)
    wkv = np.concatenate([wkv[..., 0:P].reshape(2, P, 1024), wkv[..., P:].reshape(2, P, 1024)], 2)
    c = np.ascontiguousarray
    t = {
        "x": c(i["x"].reshape(T, D)),
        "even_in": feature_units(feats), "even_v": token_units(w[:, 2 * a:3 * a]),
        "even_out": token_units(i["ab_w_out"][0]),
        "odd_in": feature_units(i["c_w_in"][0][:, 0:4096]),
        "odd_v": token_units(i["c_w_in"][0][:, 4096:]),
        "odd_out": token_units(i["c_w_out"][0]),
        "w_qb": c(wq.transpose(1, 0, 2)), "w_kvb": c(wkv.transpose(1, 0, 2)),
        "q_gain": c(i["b_q_norm"][0].reshape(4, P).T), "kv_gain": c(i["b_kv_norm"][0].reshape(2, P).T),
        "keys_t": c(i["peer_sub_keys"].reshape(2, 16, N_KEYS, P).transpose(0, 3, 1, 2)),
        "ln_gain": c(i["ln_gain"].reshape(4, D)), "ln_bias": c(i["ln_bias"].reshape(4, D)),
    }
    for n in range(2):
        t[f"query{n}"] = feature_units(i["peer_w_query"][n])
        u = i["peer_u"][n].reshape(P, P, 2, 8, P)
        t[f"u{n}"] = c(u.transpose(1, 2, 4, 3, 0)).reshape(2 * P, P, UNIT)
        v = i["peer_v"][n].reshape(P, P, 2, UNIT)
        t[f"v{n}"] = c(v.transpose(1, 2, 0, 3)).reshape(2 * P, P, UNIT)
    t.update(shape_constants())
    return t


def kernel(**inputs):
    import concourse.bacc as bacc
    from concourse.bass_utils import run_bass_kernel_spmd

    nc = bacc.Bacc("TRN2", target_bir_lowering=False, num_devices=1)
    arrays = layout(inputs)
    t = {}
    for name, a in arrays.items():
        t[name] = nc.dram_tensor(f"in_{name}", a.shape, mybir.dt.from_np(a.dtype),
                                 kind="ExternalInput").ap()
    t["kept"] = nc.dram_tensor("kept", (3, T, D), F32).ap()
    t["out"] = nc.dram_tensor("out_x", (T, D), F32, kind="ExternalOutput").ap()
    decoder(nc, t)
    r = run_bass_kernel_spmd(nc, [{f"in_{name}": a for name, a in arrays.items()}], core_ids=[0])
    return r.results[0]["out_x"].reshape(1, T, D)
```
